# Optimizing a Trainium2 kernel written in Bass

```python
import jax, jax.numpy as jnp
from jax import lax
import numpy as np

D_MODEL = 2048
BATCH = 1
SEQ = 1024
DEPTH = 1

D_MIX = D_MODEL
D_CONV = D_MIX // 2
CONV_GROUPS = 8
CONV_WIDTH = 31
D_SSD = D_MIX - D_CONV
SSD_HEAD_DIM = 64
SSD_HEADS = D_SSD // SSD_HEAD_DIM
SSD_GROUPS = 2
SSD_STATE = 128
SSD_CONV_WIDTH = 4
SSD_CHUNK = 128
SSD_XBC = D_SSD + 2 * SSD_GROUPS * SSD_STATE
D_IN_TOTAL = 2 * D_CONV + D_SSD + SSD_XBC + SSD_HEADS
N_EXPERTS = 32
N_EXPERT_GROUPS = 8
EXPERTS_PER_GROUP = N_EXPERTS // N_EXPERT_GROUPS
TOP_K = 2
D_EXPERT = 512
MOE_BLOCK = 128
EPS = 1e-6

kernel_name = "hymba_conformer_ssd_grouped_moe_adaln"

def rms_norm(x, w):
    xf = x.astype(jnp.float32)
    y = xf * lax.rsqrt(jnp.mean(xf * xf, axis=-1, keepdims=True) + EPS)
    return (y * w.astype(jnp.float32)).astype(x.dtype)

def modulate(h, shift, scale):
    return h * (1 + scale[:, None, :]) + shift[:, None, :]

def causal_depthwise_conv(x, w, b):
    k, ch = w.shape
    y = lax.conv_general_dilated(
        x, w[:, None, :].astype(x.dtype), window_strides=(1,),
        padding=((k - 1, 0),), dimension_numbers=("NWC", "WIO", "NWC"),
        feature_group_count=ch)
    return y + b.astype(x.dtype)

def conformer_conv_group(a, g, dw_w, dw_b, ln_w, ln_b):
    u = a * jax.nn.sigmoid(g)
    u = causal_depthwise_conv(u, dw_w, dw_b)
    bsz, seq, ch = u.shape
    uf = u.astype(jnp.float32).reshape(bsz, seq, CONV_GROUPS, ch // CONV_GROUPS)
    mu = jnp.mean(uf, axis=-1, keepdims=True)
    var = jnp.mean(jnp.square(uf - mu), axis=-1, keepdims=True)
    uf = ((uf - mu) * lax.rsqrt(var + EPS)).reshape(bsz, seq, ch)
    uf = uf * ln_w.astype(jnp.float32) + ln_b.astype(jnp.float32)
    return jax.nn.silu(uf).astype(a.dtype)

def segsum(a):
    cs = jnp.cumsum(a, axis=-1)
    diff = cs[..., :, None] - cs[..., None, :]
    t = a.shape[-1]
    mask = jnp.tril(jnp.ones((t, t), dtype=bool))
    return jnp.where(mask, diff, -jnp.inf)

def ssd_chunked_scan(x, dt, a, bm, cm):
    bsz, seq, nh, hp = x.shape
    ng, ns = bm.shape[-2:]
    r = nh // ng
    q = SSD_CHUNK
    nc = seq // q
    xd = (x.astype(jnp.float32) * dt[..., None]).reshape(bsz, nc, q, ng, r, hp)
    da = (dt * a).reshape(bsz, nc, q, ng, r).transpose(0, 3, 4, 1, 2)
    bm = bm.astype(jnp.float32).reshape(bsz, nc, q, ng, ns)
    cm = cm.astype(jnp.float32).reshape(bsz, nc, q, ng, ns)
    da_cs = jnp.cumsum(da, axis=-1)
    decay_in = jnp.exp(segsum(da))
    cb = jnp.einsum("bclgn,bcsgn->bcgls", cm, bm)
    y_diag = jnp.einsum("bcgls,bgrcls,bcsgrp->bclgrp", cb, decay_in, xd)
    decay_states = jnp.exp(da_cs[..., -1:] - da_cs)
    states = jnp.einsum("bclgn,bgrcl,bclgrp->bcgrpn", bm, decay_states, xd)
    chunk_decay = jnp.exp(da_cs[..., -1])

    def step(h, inp):
        s_c, d_c = inp
        return h * d_c[..., None, None] + s_c, h

    h0 = jnp.zeros((bsz, ng, r, hp, ns), jnp.float32)
    _, prev = lax.scan(step, h0, (states.transpose(1, 0, 2, 3, 4, 5),
                                  chunk_decay.transpose(3, 0, 1, 2)))
    prev = prev.transpose(1, 0, 2, 3, 4, 5)
    y_off = jnp.einsum("bclgn,bcgrpn,bgrcl->bclgrp", cm, prev, jnp.exp(da_cs))
    return (y_diag + y_off).reshape(bsz, seq, nh, hp)

def ssd_group(z, xbc, dt_raw, conv_w, conv_b, a_log, dt_bias, d_skip, norm_w):
    bsz, seq, _ = z.shape
    gn = SSD_GROUPS * SSD_STATE
    xbc = jax.nn.silu(causal_depthwise_conv(xbc, conv_w, conv_b))
    xs = xbc[..., :D_SSD].reshape(bsz, seq, SSD_HEADS, SSD_HEAD_DIM)
    bm = xbc[..., D_SSD:D_SSD + gn].reshape(bsz, seq, SSD_GROUPS, SSD_STATE)
    cm = xbc[..., D_SSD + gn:].reshape(bsz, seq, SSD_GROUPS, SSD_STATE)
    dt = jax.nn.softplus(dt_raw.astype(jnp.float32) + dt_bias.astype(jnp.float32))
    a = -jnp.exp(a_log.astype(jnp.float32))
    y = ssd_chunked_scan(xs, dt, a, bm, cm)
    y = y + d_skip.astype(jnp.float32)[:, None] * xs.astype(jnp.float32)
    y = y.reshape(bsz, seq, D_SSD) * jax.nn.silu(z.astype(jnp.float32))
    yg = y.reshape(bsz, seq, SSD_GROUPS, D_SSD // SSD_GROUPS)
    yg = yg * lax.rsqrt(jnp.mean(yg * yg, axis=-1, keepdims=True) + EPS)
    return (yg.reshape(bsz, seq, D_SSD) * norm_w.astype(jnp.float32)).astype(z.dtype)

def grouped_route(h2d, w_router, router_bias):
    t = h2d.shape[0]
    s = jax.nn.sigmoid((h2d @ w_router).astype(jnp.float32))
    s_sel = s + router_bias.astype(jnp.float32)
    grp = s_sel.reshape(t, N_EXPERT_GROUPS, EXPERTS_PER_GROUP)
    grp_score = jnp.sum(lax.top_k(grp, TOP_K)[0], axis=-1)
    best = jnp.argmax(grp_score, axis=-1)
    keep = jnp.arange(N_EXPERT_GROUPS)[None, :] == best[:, None]
    masked = jnp.where(keep[..., None], grp, -jnp.inf).reshape(t, N_EXPERTS)
    _, idx = lax.top_k(masked, TOP_K)
    gw = jnp.take_along_axis(s, idx, axis=-1)
    gw = gw / jnp.sum(gw, axis=-1, keepdims=True)
    return idx, gw

def routed_experts(h2d, idx, gw, w_gate, w_up, w_down):
    t, d = h2d.shape
    n_assign = t * TOP_K
    e_flat = idx.reshape(n_assign)
    tok_flat = jnp.arange(n_assign) // TOP_K
    g_flat = gw.reshape(n_assign)
    order = jnp.argsort(e_flat)
    e_sorted, tok_sorted, g_sorted = e_flat[order], tok_flat[order], g_flat[order]
    counts = jnp.bincount(e_flat, length=N_EXPERTS)
    starts = jnp.cumsum(counts) - counts
    padded = ((counts + MOE_BLOCK - 1) // MOE_BLOCK) * MOE_BLOCK
    pends = jnp.cumsum(padded)
    pstarts = pends - padded
    dest = pstarts[e_sorted] + (jnp.arange(n_assign) - starts[e_sorted])
    n_blocks = n_assign // MOE_BLOCK + N_EXPERTS
    buf = jnp.zeros((n_blocks * MOE_BLOCK, d), h2d.dtype).at[dest].set(h2d[tok_sorted])
    block_expert = jnp.minimum(
        jnp.searchsorted(pends, jnp.arange(n_blocks) * MOE_BLOCK, side="right"),
        N_EXPERTS - 1)

    def expert_block(args):
        xb, e = args
        hb = jax.nn.silu(xb @ w_gate[e]) * (xb @ w_up[e])
        return hb @ w_down[e]

    out = lax.map(expert_block, (buf.reshape(n_blocks, MOE_BLOCK, d), block_expert))
    out = out.reshape(n_blocks * MOE_BLOCK, d)
    contrib = out[dest] * g_sorted[:, None].astype(out.dtype)
    return jnp.zeros((t, d), h2d.dtype).at[tok_sorted].add(contrib)

def hybrid_layer(x, c_act, w_mod, b_mod, norm1_w, w_in, conv_dw_w, conv_dw_b,
                 conv_ln_w, conv_ln_b, ssd_conv_w, ssd_conv_b, a_log, dt_bias,
                 d_skip, ssd_norm_w, w_out, norm2_w, w_router, router_bias,
                 w_gate, w_up, w_down):
    bsz, seq, d = x.shape
    mod = c_act @ w_mod + b_mod
    sh1, sc1, g1, sh2, sc2, g2 = jnp.split(mod, 6, axis=-1)
    h = modulate(rms_norm(x, norm1_w), sh1, sc1)
    proj = h @ w_in
    cuts = [D_CONV, 2 * D_CONV, 2 * D_CONV + D_SSD, 2 * D_CONV + D_SSD + SSD_XBC]
    conv_a, conv_g, z, xbc, dt_raw = jnp.split(proj, cuts, axis=-1)
    y_conv = conformer_conv_group(conv_a, conv_g, conv_dw_w, conv_dw_b, conv_ln_w, conv_ln_b)
    y_ssd = ssd_group(z, xbc, dt_raw, ssd_conv_w, ssd_conv_b, a_log, dt_bias, d_skip, ssd_norm_w)
    mix = jnp.concatenate([y_conv, y_ssd], axis=-1) @ w_out
    x = x + g1[:, None, :] * mix
    h = modulate(rms_norm(x, norm2_w), sh2, sc2).reshape(bsz * seq, d)
    idx, gw = grouped_route(h, w_router, router_bias)
    y = routed_experts(h, idx, gw, w_gate, w_up, w_down).reshape(bsz, seq, d)
    return x + g2[:, None, :] * y

def setup_inputs(seed: int = 0) -> dict:
    key = jax.random.key(seed)
    ks = jax.random.split(key, 26)
    f32 = jnp.float32
    n = lambda k, s, sc: jax.random.normal(k, s, f32) * sc
    gn = SSD_GROUPS * SSD_STATE
    dt0 = jnp.exp(jax.random.uniform(ks[13], (DEPTH, SSD_HEADS), f32)
                  * (np.log(0.1) - np.log(1e-3)) + np.log(1e-3))
    return {
        "x": n(ks[0], (BATCH, SEQ, D_MODEL), 1.0),
        "c": n(ks[1], (BATCH, D_MODEL), 1.0),
        "w_mod": n(ks[2], (DEPTH, D_MODEL, 6 * D_MODEL), 0.5 * D_MODEL ** -0.5),
        "b_mod": n(ks[3], (DEPTH, 6 * D_MODEL), 0.02),
        "norm1_w": 1.0 + n(ks[4], (DEPTH, D_MODEL), 0.02),
        "w_in": n(ks[5], (DEPTH, D_MODEL, D_IN_TOTAL), D_MODEL ** -0.5),
        "conv_dw_w": n(ks[6], (DEPTH, CONV_WIDTH, D_CONV), CONV_WIDTH ** -0.5),
        "conv_dw_b": n(ks[7], (DEPTH, D_CONV), 0.02),
        "conv_ln_w": 1.0 + n(ks[8], (DEPTH, D_CONV), 0.02),
        "conv_ln_b": n(ks[9], (DEPTH, D_CONV), 0.02),
        "ssd_conv_w": n(ks[10], (DEPTH, SSD_CONV_WIDTH, SSD_XBC), SSD_CONV_WIDTH ** -0.5),
        "ssd_conv_b": n(ks[11], (DEPTH, SSD_XBC), 0.02),
        "a_log": jnp.log(jax.random.uniform(ks[12], (DEPTH, SSD_HEADS), f32, 1.0, 16.0)),
        "dt_bias": dt0 + jnp.log(-jnp.expm1(-dt0)),
        "d_skip": 1.0 + n(ks[14], (DEPTH, SSD_HEADS), 0.02),
        "ssd_norm_w": 1.0 + n(ks[15], (DEPTH, D_SSD), 0.02),
        "w_out": n(ks[16], (DEPTH, D_MIX, D_MODEL), D_MIX ** -0.5),
        "norm2_w": 1.0 + n(ks[17], (DEPTH, D_MODEL), 0.02),
        "w_router": n(ks[18], (D_MODEL, N_EXPERTS), D_MODEL ** -0.5),
        "router_bias": n(ks[19], (N_EXPERTS,), 0.01),
        "w_gate": n(ks[20], (DEPTH, N_EXPERTS, D_MODEL, D_EXPERT), D_MODEL ** -0.5),
        "w_up": n(ks[21], (DEPTH, N_EXPERTS, D_MODEL, D_EXPERT), D_MODEL ** -0.5),
        "w_down": n(ks[22], (DEPTH, N_EXPERTS, D_EXPERT, D_MODEL), D_EXPERT ** -0.5),
        "final_norm_w": 1.0 + n(ks[23], (D_MODEL,), 0.02),
    }

def reference(x, c, w_mod, b_mod, norm1_w, w_in, conv_dw_w, conv_dw_b, conv_ln_w,
              conv_ln_b, ssd_conv_w, ssd_conv_b, a_log, dt_bias, d_skip, ssd_norm_w,
              w_out, norm2_w, w_router, router_bias, w_gate, w_up, w_down,
              final_norm_w):
    c_act = jax.nn.silu(c)
    for i in range(DEPTH):
        x = hybrid_layer(x, c_act, w_mod[i], b_mod[i], norm1_w[i], w_in[i],
                         conv_dw_w[i], conv_dw_b[i], conv_ln_w[i], conv_ln_b[i],
                         ssd_conv_w[i], ssd_conv_b[i], a_log[i], dt_bias[i],
                         d_skip[i], ssd_norm_w[i], w_out[i], norm2_w[i],
                         w_router, router_bias, w_gate[i], w_up[i], w_down[i])
    return rms_norm(x, final_norm_w)


_drawn_inputs = setup_inputs


def setup_inputs(seed=0):
    import zlib

    import numpy as np

    out = dict(_drawn_inputs(seed))
    spreads = {}
    factors = {'norm1_w': 3.723,
     'conv_dw_b': 13.842,
     'conv_ln_w': 21.635,
     'conv_ln_b': 23.286,
     'ssd_conv_b': 10.229,
     'd_skip': 51.264,
     'ssd_norm_w': 18.681,
     'final_norm_w': 8.13,
     'norm2_w': 4.422}
    for name, (base, spread) in spreads.items():
        noise = np.random.default_rng([zlib.crc32(name.encode()), seed]).standard_normal(out[name].shape)
        drawn = base * np.exp(spread * noise) if base else spread * noise
        out[name] = __import__('jax').numpy.asarray(drawn.astype(out[name].dtype))
    for name, factor in factors.items():
        out[name] = (out[name] * factor).astype(out[name].dtype)
    return out
```

```python
from contextlib import ExitStack

import numpy as np
import concourse.bass as bass
from concourse import mybir

F32 = mybir.dt.float32
U32 = mybir.dt.uint32
I32 = mybir.dt.int32
F32R = mybir.dt.float32r
ALU = mybir.AluOpType
ACT = mybir.ActivationFunctionType
X = mybir.AxisListType.X
ds = bass.ds

P = 128
D = 2048
KT = D // P
SEQ = 1024
TT = SEQ // P
DC = 1024
DS = 1024
CT = DC // P
TAPS = 31
STAPS = 4
XBC = DS + 4 * P
XT = XBC // P
H = 16
HD = 64
COL_G, COL_Z, COL_XBC, COL_DT = DC, 2 * DC, 2 * DC + DS, 2 * DC + DS + XBC
E = 32
G = 8
FE = 512
FT = FE // P
BLK = 128
MAX_ITEMS = 2 * SEQ // BLK + E - 1
EPS = 1e-6
BIG = 1e30
V_TAP, V_CB, V_LNW, V_LNB, V_STAP, V_SB, V_SNW, V_D, NV = 0, 31, 32, 33, 34, 38, 39, 40, 41


class Order:

    def __init__(self, eng, sem, base=0):
        self.eng, self.sem, self.base, self.n = eng, sem, base, 0

    def __call__(self, ins):
        self.n += 1
        ins.then_inc(self.sem, 1)
        self.eng.wait_ge(self.sem, self.base + self.n)


def hybrid_layer(nc, x, c, w_mod, b_mod, norm1_w, w_in, conv_dw_w, conv_dw_b, conv_ln_w, conv_ln_b,
                 ssd_conv_w, ssd_conv_b, a_log, dt_bias, d_skip, ssd_norm_w, w_out, norm2_w,
                 w_router, router_bias, w_gate, w_up, w_down, final_norm_w, out):
    x, out = x[0], out[0]
    w_mod, w_in, w_out = w_mod[0], w_in[0], w_out[0]
    w_gate, w_up, w_down = w_gate[0], w_up[0], w_down[0]

    def scratch(name, shape, dt=F32):
        return nc.dram_tensor(name, shape, dt, kind="Internal").ap()

    ycv_d = scratch("ycv_d", (CT, P, SEQ))
    zs_d = scratch("zs_d", (CT, P, SEQ))
    xbc_d = scratch("xbc_d", (XT, P, SEQ))
    modp_d = scratch("modp_d", (2, P, 1024))
    modq_d = scratch("modq_d", (3, P, D))
    x1_d = scratch("x1_d", (SEQ, D))
    h2_d = scratch("h2_d", (SEQ, D))
    tok_d = scratch("tok_d", (2 * SEQ + BLK, 1), U32)
    ybuf_d = scratch("ybuf_d", (2 * SEQ + BLK, D))
    items_d = scratch("items_d", (P, 2), I32)
    nitems_d = scratch("nitems_d", (1, 2), I32)

    top = ExitStack()
    sems = {}

    def sem(name):
        assert name not in sems
        sems[name] = nc.alloc_semaphore(name=name)
        return sems[name]

    def retire_semaphores():
        nc.clear_and_free_semaphores(list(sems.values()))
        nc.all_engine_barrier()
        sems.clear()

    def sb(stack, name, shape, dt=F32):
        return stack.enter_context(nc.sbuf_tensor(name, shape, dt))

    def row_of(v):
        return v.rearrange("(a n) -> a n", a=1) if len(v.shape) == 1 else v

    def bcast(v, n):
        return row_of(v).broadcast_to((P, n))

    with top:
        ps = top.enter_context(nc.psum_tensor("ps", [P, 8 * 512], F32))
        ident = sb(top, "ident", [P, P])
        ones = sb(top, "ones", [P, P])
        mean = sb(top, "mean", [P, P])
        tri = sb(top, "tri", [P, P])
        tris = sb(top, "tris", [P, P])
        epsc = sb(top, "epsc", [P, 1])
        vecs = sb(top, "vecs", [P, XT, NV])
        dtt = sb(top, "dtt", [P, TT, H])
        da = sb(top, "da", [P, TT, H])
        dest = sb(top, "dest", [P, TT, 2], U32)
        gw = sb(top, "gw", [P, TT, 2])
        ssqp = sb(top, "ssqp", [P, TT, 4])
        cact = sb(top, "cact", [P, KT])

        ph01 = ExitStack()
        h_at = nc.sbuf_base
        hT = sb(ph01, "hT", [P, KT, SEQ])
        hl = nc.alloc_sbuf_tensor_at("hl", [P, KT, SEQ], F32R, offset=h_at)
        sh1 = sb(ph01, "sh1", [P, KT])
        sc1 = sb(ph01, "sc1", [P, KT])
        s_const = sem("const_ready")
        with ExitStack() as st:
            xin = sb(st, "xin", [P, 2, D])
            junk = sb(st, "junk", [P, D])
            xn = sb(st, "xn", [P, D])
            ssq = sb(st, "ssq", [P, TT])
            std = sb(st, "std", [P, TT])
            rstd = sb(st, "rstd", [P, TT])
            wm = sb(st, "wm", [P, 4, 2 * D])
            macc = sb(st, "macc", [P, 2 * D])
            ccol = sb(st, "ccol", [P, KT])
            bcol = sb(st, "bcol", [P, 2, KT])
            n1col = sb(st, "n1col", [P, KT])
            vrow = sb(st, "vrow", [V_D, XBC])
            dsk = sb(st, "dsk", [P, H])
            s_col, s_vrow, s_vz = sem("columns_loaded"), sem("vrow_loaded"), sem("vrow_zeroed")
            s_cact = sem("c_activated")
            s_x = [sem(f"x_loaded{b}") for b in range(2)]
            s_wm = [sem(f"wmod_loaded{q}") for q in range(4)]
            s_wmfree = [sem(f"wmod_summed{q}") for q in range(4)]
            s_std, s_sqd, s_xn, s_xtr, s_xev = (sem("x_std"), sem("x_squared"), sem("x_normed"),
                                                sem("x_transposed"), sem("x_evacuated"))
            s_macc, s_mcol, s_vtr, o_p0 = (sem("macc_zeroed"), sem("mod_columns"),
                                           sem("vecs_transposed"), sem("p0_order"))
            wm_v = w_mod.rearrange("(p t) n -> t p n", t=KT)
            with nc.Block() as block:
                @block.gpsimd
                def _(pool):
                    pool.memset(vrow[:], 0.0).then_inc(s_vz, 1)
                    pool.memset(ident[:], 0.0).then_inc(s_const, 1)
                    pool.memset(ones[:], 1.0).then_inc(s_const, 1)
                    pool.memset(mean[:], 1.0 / P).then_inc(s_const, 1)
                    pool.memset(tri[:], 1.0).then_inc(s_const, 1)
                    pool.memset(tris[:], 1.0).then_inc(s_const, 1)
                    pool.memset(epsc[:], EPS).then_inc(s_const, 1)
                    pool.memset(vecs[:], 0.0).then_inc(s_const, 1)
                    pool.wait_ge(s_const, 7)
                    pool.affine_select(out=ident[:], in_=ident[:], compare_op=ALU.not_equal, fill=1.0,
                                       base=0, pattern=[[-1, P]], channel_multiplier=1).then_inc(s_const, 1)
                    pool.affine_select(out=tri[:], in_=tri[:], compare_op=ALU.is_ge, fill=0.0,
                                       base=0, pattern=[[1, P]], channel_multiplier=-1).then_inc(s_const, 1)
                    pool.affine_select(out=tris[:], in_=tris[:], compare_op=ALU.is_gt, fill=0.0,
                                       base=0, pattern=[[1, P]], channel_multiplier=-1).then_inc(s_const, 1)

                @block.sync
                def _(sp):
                    with sp.Fori(0, KT // 4) as i:
                        for q in range(4):
                            sp.wait_ge(s_wmfree[q], i)
                            sp.dma_start(wm[:, q, :], wm_v[ds(4 * i + q, 1), :, 0:2 * D].rearrange("a p n -> (a p) n")
                                         ).then_inc(s_wm[q], 16)

                @block.scalar
                def _(act):
                    act.dma_start(ccol[:], c.rearrange("a (p t) -> (a p) t", t=KT)).then_inc(s_col, 16)
                    act.dma_start(bcol[:, 0, :], b_mod[0, 0:D].rearrange("(p t) -> p t", t=KT)).then_inc(s_col, 16)
                    act.dma_start(bcol[:, 1, :], b_mod[0, D:2 * D].rearrange("(p t) -> p t", t=KT)).then_inc(s_col, 16)
                    act.dma_start(n1col[:], norm1_w[0].rearrange("(p t) -> p t", t=KT)).then_inc(s_col, 16)
                    act.wait_ge(s_vz, 1)
                    rows = [(V_TAP, TAPS, DC, conv_dw_w[0]), (V_CB, 1, DC, conv_dw_b), (V_LNW, 1, DC, conv_ln_w),
                            (V_LNB, 1, DC, conv_ln_b), (V_STAP, STAPS, XBC, ssd_conv_w[0]), (V_SB, 1, XBC, ssd_conv_b),
                            (V_SNW, 1, DS, ssd_norm_w)]
                    for r, n, w, src in rows:
                        act.dma_start(vrow[r:r + n, 0:w], src).then_inc(s_vrow, 16)
                    act.dma_start(dsk[:], bcast(d_skip, H)).then_inc(s_vrow, 16)
                    act.wait_ge(s_col, 64)
                    act.activation(cact[:], ccol[:], ACT.Silu).then_inc(s_cact, 1)
                    act.wait_ge(s_const, 10)
                    with act.Fori(0, TT // 2) as i:
                        for b in range(2):
                            act.wait_ge(s_xn, 2 * i)
                            act.dma_start(xin[:, b, :], x[ds((2 * i + b) * P, P), :]).then_inc(s_x[b], 16)
                        for b in range(2):
                            j = 2 * i + b
                            act.wait_ge(s_x[b], 16 * i + 16)
                            act.activation(junk[:], xin[:, b, :], ACT.Square,
                                           accum_out=ssq[:, ds(j, 1)]).then_inc(s_sqd, 1)
                            act.wait_ge(s_sqd, j + 1)
                            act.activation(std[:, ds(j, 1)], ssq[:, ds(j, 1)], ACT.Sqrt, bias=epsc[:],
                                           scale=1.0 / D).then_inc(s_std, 1)
                            for q in range(4):
                                act.wait_ge(s_xtr, 4 * j + q + 1)
                                act.activation(hT[:, 4 * q:4 * q + 4, ds(j * P, P)],
                                               ps[:, 512 * q:512 * q + 512].rearrange("p (a b) -> p a b", b=P),
                                               ACT.Copy).then_inc(s_xev, 1)

                @block.vector
                def _(dve):
                    dve.memset(macc[:], 0.0).then_inc(s_macc, 1)
                    dve.wait_ge(s_macc, 1)
                    dve.wait_ge(s_cact, 1)
                    with dve.Fori(0, TT // 2) as i:
                        order = Order(dve, o_p0, i * 2)
                        for b in range(2):
                            j = 2 * i + b
                            for q in (2 * b, 2 * b + 1):
                                dve.wait_ge(s_wm[q], 16 * i + 16)
                                dve.scalar_tensor_tensor(out=macc[:], in0=wm[:, q, :], scalar=cact[:, ds(4 * i + q, 1)],
                                                         in1=macc[:], op0=ALU.mult, op1=ALU.add).then_inc(s_wmfree[q], 1)
                                dve.wait_ge(s_wmfree[q], i + 1)
                            dve.wait_ge(s_std, j + 1)
                            order(dve.reciprocal(rstd[:, ds(j, 1)], std[:, ds(j, 1)]))
                            dve.wait_ge(s_xtr, 4 * j)
                            dve.tensor_scalar(xn[:], xin[:, b, :], rstd[:, ds(j, 1)], None, ALU.mult).then_inc(s_xn, 1)
                    order = Order(dve, o_p0, TT)
                    dve.wait_ge(s_vtr, 1)
                    dve.tensor_copy(vecs[:, :, 0:V_D], ps[:, 2560:2560 + XT * V_D].rearrange("p (a b) -> p a b", b=V_D))
                    for r in range(2):
                        dve.tensor_copy(vecs[HD * r:HD * r + HD, 0:CT, V_D],
                                        dsk[HD * r:HD * r + HD, :].rearrange("p (q r) -> p r q", r=2)[:, r, :])
                    dve.wait_ge(s_mcol, 1)
                    order(dve.tensor_tensor(sh1[:], ps[:, 2048:2048 + KT], bcol[:, 0, :], ALU.add))
                    order(dve.tensor_tensor(sc1[:], ps[:, 2048 + KT:2048 + 2 * KT], bcol[:, 1, :], ALU.add))
                    order(dve.scalar_tensor_tensor(out=sc1[:], in0=sc1[:], scalar=1.0, in1=n1col[:],
                                                   op0=ALU.add, op1=ALU.mult))

                @block.tensor
                def _(pe):
                    pe.wait_ge(s_const, 10)
                    pe.wait_ge(s_vrow, 8 * 16)
                    for ct in range(XT):
                        last = pe.transpose(ps[:, 2560 + ct * V_D:2560 + (ct + 1) * V_D],
                                            vrow[:, ct * P:(ct + 1) * P], ident[0:V_D, 0:V_D])
                    last.then_inc(s_vtr, 1)
                    with pe.Fori(0, TT) as j:
                        pe.wait_ge(s_xn, j + 1)
                        for q in range(4):
                            pe.wait_ge(s_xev, 4 * j)
                            for a in range(4):
                                t = 4 * q + a
                                last = pe.transpose(ps[:, t * P:(t + 1) * P],
                                                    xn[:].rearrange("p (m t) -> p t m", t=KT)[:, t, :], ident[:])
                            last.then_inc(s_xtr, 1)
                    pe.wait_ge(s_wmfree[3], KT // 4)
                    mv = macc[:].rearrange("p (v m t) -> p v t m", v=2, t=KT)
                    for v in range(2):
                        for t in range(KT):
                            last = pe.matmul(ps[:, 2048 + v * KT + t:2049 + v * KT + t], mv[:, v, t, :],
                                             ones[:, 0:1], start=True, stop=True)
                    last.then_inc(s_mcol, 1)

        NA, NB = CT, XT // 3
        ROWS, AHEAD = (0, 10, 21, 2 * KT), 4
        with ExitStack() as st:
            hh = sb(st, "hh", [P, KT, SEQ], F32R)
            wraw_i = sb(st, "wraw_i", [P, 3, 8, P])
            wih = sb(st, "wih", [P, 3, 8, P], F32R)
            wil = sb(st, "wil", [P, 3, 8, P], F32R)
            wm2 = sb(st, "wm2", [P, 2, 1024])
            macc2 = sb(st, "macc2", [P, 1024])
            sg = sb(st, "sg", [P, SEQ])
            u = sb(st, "u", [P, TAPS - 1 + SEQ])
            acc = sb(st, "acc", [P, SEQ])
            dd = sb(st, "dd", [P, SEQ])
            sq = sb(st, "sq", [P, SEQ])
            xpad = sb(st, "xpad", [P, STAPS - 1 + SEQ])
            vcur = sb(st, "vcur", [P, NV])
            vcur3 = sb(st, "vcur3", [P, 3, NV])
            wdh = wih[:, 0, 0:2, :].rearrange("p a (t h) -> p (a t) h", h=H)
            wdl = wil[:, 0, 0:2, :].rearrange("p a (t h) -> p (a t) h", h=H)
            wdt = dd[:, 5 * TT * H:5 * TT * H + KT * H].rearrange("p (t h) -> p t h", h=H)
            dtb = sb(st, "dtb", [P, H])
            acol = sb(st, "acol", [P, H])
            dx = [dd[:, TT * H * n:TT * H * (n + 1)].rearrange("p (j h) -> p j h", h=H) for n in range(5)]
            s_w = [sem(f"w_in_loaded{s}") for s in range(3)]
            s_wr, s_wsp = sem("w_in_rounded"), [sem(f"w_in_split{s}") for s in range(3)]
            s_wu = [sem(f"w_in_used{s}") for s in range(3)]
            s_mt, s_mh, s_ml, s_wdr, s_wds = (sem("h_modulated"), sem("h_rounded"), sem("h_split"),
                                              sem("w_dt_rounded"), sem("w_dt_split"))
            mslot = [wm2[:, 0, :], wm2[:, 1, :], sq[:], u[:, TAPS - 1:]]
            s_wm2 = [sem(f"wmod2_loaded{b}") for b in range(4)]
            s_wm2u = [sem(f"wmod2_summed{b}") for b in range(4)]
            s_dtl, s_sig, s_u, s_z, s_conv = (sem("dt_inputs_loaded"), sem("g_sigmoid"), sem("u_ready"),
                                              sem("z_silu"), sem("conv_done"))
            s_mean, s_d, s_sq, s_var, s_sd, s_nrm = (sem("mean_done"), sem("centred"), sem("squared"),
                                                     sem("var_done"), sem("sd_done"), sem("normed"))
            s_y, s_zs, s_ys, s_ms = sem("conv_out"), sem("z_stored"), sem("y_stored"), sem("modp_stored")
            s_pad, s_dtc, s_dtt = sem("xbc_padded"), sem("dt_copied"), sem("dt_transposed")
            s_cb, s_xo, s_xs = sem("xbc_conv_done"), sem("xbc_silu"), sem("xbc_stored")
            s_pz, s_dtp, s_dx, s_de, o_p1, o_p1b, o_p1c = (sem("pads_zeroed"), sem("dt_projected"), sem("dt_exp_in"),
                                                    sem("dt_exp_out"), sem("p1a_order"), sem("p1b_order"), sem("p1c_order"))
            wi_v = w_in.rearrange("(p t) n -> p t n", t=KT)
            wm2_v = w_mod.rearrange("(p t) n -> p t n", t=KT)
            with nc.Block() as block:
                @block.sync
                def _(sp):
                    sp.dma_start(dtb[:], bcast(dt_bias, H)).then_inc(s_dtl, 16)
                    sp.dma_start(acol[:], bcast(a_log, H)).then_inc(s_dtl, 16)

                    def load(r, q, col, it):
                        k = 2 * r + q
                        if not isinstance(col, int):
                            sp.lower_val(col * 4)
                        sp.wait_ge(s_wsp[k % 3], 2 * it + k // 3)
                        sp.dma_start(wraw_i[:, k % 3, :, :], wi_v[:, 8 * q:8 * q + 8, ds(col, P)]).then_inc(s_w[k % 3], 16)

                    with sp.Fori(0, NA) as it:
                        for r, base in enumerate((COL_G, 0, COL_Z)):
                            for q in range(2):
                                load(r, q, it * P + base, it)
                    for r in range(3):
                        for q in range(2):
                            load(r, q, COL_XBC + r * P, NA)
                    with sp.Fori(1, NB) as it:
                        for r in range(3):
                            for q in range(2):
                                load(r, q, it * (3 * P) + (COL_XBC + r * P), it + NA)

                @block.gpsimd
                def _(pool):
                    pool.memset(u[:, 0:TAPS - 1], 0.0).then_inc(s_pz, 1)
                    pool.memset(xpad[:, 0:STAPS - 1], 0.0).then_inc(s_pz, 1)
                    with pool.Fori(0, NA + NB) as it:
                        for k in range(6):
                            s = k % 3
                            pool.wait_ge(s_w[s], 32 * it + 16 * (k // 3) + 16)
                            pool.wait_ge(s_wu[s], 2 * it + k // 3)
                            pool.tensor_tensor(wih[:, s, :, :], wraw_i[:, s, :, :], ones[:, None, :].broadcast_to((P, 8, P)), ALU.mult).then_inc(s_wr, 1)
                            pool.wait_ge(s_wr, 6 * it + k + 1)
                            pool.tensor_tensor(wil[:, s, :, :], wraw_i[:, s, :, :], wih[:, s, :, :].bitcast(F32),
                                               ALU.subtract).then_inc(s_wsp[s], 1)
                    pool.wait_ge(s_dtl, 48)
                    pool.wait_ge(s_wu[0], 2 * (NA + NB))
                    pool.tensor_copy(wdh, wdt).then_inc(s_wdr, 1)
                    pool.wait_ge(s_wdr, 1)
                    pool.tensor_tensor(wdl, wdt, wdh.bitcast(F32), ALU.subtract).then_inc(s_wds, 1)

                def tile_done(eng, r, it):
                    k = 2 * r + 1
                    eng.wait_ge(s_wu[k % 3], 2 * it + k // 3 + 1)

                def proj(pe, r, it, begin=False):
                    for q in range(2):
                        s = (2 * r + q) % 3
                        pe.wait_ge(s_wsp[s], 2 * it + (2 * r + q) // 3 + 1)
                        for k in range(8):
                            t = 8 * q + k
                            if begin:
                                pe.wait_ge(s_ml, t + 1)
                            for n, (w, x_) in enumerate(((wih, hh), (wih, hl), (wil, hh))):
                                for h in range(2):
                                    last = pe.matmul(ps[:, 1024 * r + 512 * h:1024 * r + 512 * h + 512], w[:, s, k, :],
                                                     x_[:, t, 512 * h:512 * h + 512],
                                                     start=(t == 0 and n == 0), stop=(t == KT - 1 and n == 2))
                        last.then_inc(s_wu[s], 1)

                def stat(pe, src, done):
                    for h in range(2):
                        last = pe.matmul(ps[:, 3072 + 512 * h:3584 + 512 * h], mean[:], src[:, 512 * h:512 * h + 512],
                                         start=True, stop=True)
                    last.then_inc(done, 1)

                def pe_mean(pe, n):
                    pe.wait_ge(s_conv, n)
                    pe.wait_ge(s_sd, n - 1)
                    stat(pe, acc, s_mean)

                def pe_var(pe, n):
                    pe.wait_ge(s_sq, n)
                    stat(pe, sq, s_var)

                @block.tensor
                def _(pe):
                    for r in range(3):
                        proj(pe, r, 0, begin=(r == 0))
                    with pe.Fori(1, NA) as it:
                        pe.wait_ge(s_sig, it)
                        proj(pe, 0, it)
                        pe_mean(pe, it)
                        pe.wait_ge(s_u, it)
                        proj(pe, 1, it)
                        pe_var(pe, it)
                        pe.wait_ge(s_z, it)
                        proj(pe, 2, it)
                    pe.wait_ge(s_sig, NA)
                    proj(pe, 0, NA)
                    pe_mean(pe, NA)
                    pe.wait_ge(s_u, NA)
                    proj(pe, 1, NA)
                    pe_var(pe, NA)
                    pe.wait_ge(s_z, NA)
                    proj(pe, 2, NA)
                    with pe.Fori(1, NB) as it:
                        for r in range(3):
                            pe.wait_ge(s_pad, 3 * it - 2 + r)
                            proj(pe, r, it + NA)
                    pe.wait_ge(s_wds, 1)
                    pe.wait_ge(s_sd, NA)
                    for h in range(2):
                        for t in range(KT):
                            for n, (w, x_) in enumerate(((wdh, hh), (wdl, hh), (wdh, hl))):
                                last = pe.matmul(ps[0:H, 3072 + 512 * h:3584 + 512 * h], w[:, t, :],
                                                 x_[:, t, 512 * h:512 * h + 512], start=(t == 0 and n == 0),
                                                 stop=(t == KT - 1 and n == 2))
                    last.then_inc(s_dtp, 1)
                    pe.wait_ge(s_dtc, 1)
                    pe.wait_ge(s_pad, XT)
                    for j in range(TT):
                        last = pe.transpose(ps[:, j * H:(j + 1) * H], sq[0:H, j * P:(j + 1) * P], ident[0:H, 0:H])
                    last.then_inc(s_dtt, 1)

                def act_square(act, n):
                    act.wait_ge(s_d, n)
                    act.wait_ge(s_ys, 16 * (n - 1))
                    act.activation(sq[:], dd[:], ACT.Square).then_inc(s_sq, 1)

                def act_finish(act, n, tile):
                    act.wait_ge(s_var, n)
                    act.activation(sq[:], ps[:, 3072:4096], ACT.Sqrt, bias=epsc[:]).then_inc(s_sd, 1)
                    act.wait_ge(s_nrm, n)
                    act.activation(sq[:], dd[:], ACT.Silu, scale=vecs[:, tile, V_LNW:V_LNW + 1].rearrange("p a b -> p (a b)"),
                                   bias=vecs[:, tile, V_LNB:V_LNB + 1].rearrange("p a b -> p (a b)")).then_inc(s_y, 1)
                    act.wait_ge(s_y, n)
                    act.dma_start(ycv_d[tile, :, :].rearrange("a p n -> (a p) n"), sq[:]).then_inc(s_ys, 16)

                def act_gates(act, it):
                    tile_done(act, 0, it)
                    act.wait_ge(s_zs, 16 * it)
                    act.activation(sg[:], ps[:, 0:1024], ACT.Sigmoid).then_inc(s_sig, 1)

                def act_z(act, it):
                    tile_done(act, 2, it)
                    act.wait_ge(s_u, it + 1)
                    act.activation(sg[:], ps[:, 2048:3072], ACT.Silu).then_inc(s_z, 1)
                    act.wait_ge(s_z, it + 1)
                    act.dma_start(zs_d[ds(it, 1), :, :].rearrange("a p n -> (a p) n"), sg[:]).then_inc(s_zs, 16)

                def act_pad(act, r, it):
                    tile_done(act, r, it + NA)
                    act.wait_ge(s_cb, 3 * it + r)
                    act.activation(xpad[:, STAPS - 1:], ps[:, 1024 * r:1024 * r + 1024], ACT.Copy).then_inc(s_pad, 1)

                def act_mod(act, rows_):
                    for row in rows_:
                        b, t, s = row // KT, row % KT, row % 4
                        if row < 2 * KT:
                            if row >= 4:
                                act.wait_ge(s_wm2u[s], row // 4)
                            act.dma_start(mslot[s], wm2_v[:, t, b * 1024 + 2 * D:(b + 1) * 1024 + 2 * D]).then_inc(s_wm2[s], 16)
                        if row % KT == 3 and row > KT:
                            act.wait_ge(s_wm2u[3], (row - 3) // 4)
                            act.dma_start(modp_d[b - 1, :, :], macc2[:]).then_inc(s_ms, 16)

                def act_xbc(act, r, it):
                    n = 3 * it + r
                    act.wait_ge(s_cb, n + 1)
                    act.wait_ge(s_xs, 16 * n)
                    act.activation(sg[:], acc[:], ACT.Silu).then_inc(s_xo, 1)
                    act.wait_ge(s_xo, n + 1)
                    act.dma_start(xbc_d[ds(n, 1), :, :].rearrange("a p n -> (a p) n"), sg[:]).then_inc(s_xs, 16)

                @block.scalar
                def _(act):
                    for t in range(KT):
                        act.wait_ge(s_mt, t + 1)
                        act.activation(hh[:, t, :], (acc, dd)[t % 2][:], ACT.Copy).then_inc(s_mh, 1)
                    act_gates(act, 0)
                    act_z(act, 0)
                    with act.Fori(1, NA) as it:
                        act_gates(act, it)
                        act_square(act, it)
                        act_z(act, it)
                        act_finish(act, it, ds(it - 1, 1))
                    act.wait_ge(s_zs, 16 * NA)
                    act_pad(act, 0, 0)
                    act_square(act, NA)
                    act_finish(act, NA, ds(NA - 1, 1))
                    act.dma_start(wdt, wi_v[:, :, COL_DT:COL_DT + H], allow_slow_non_contiguous=True).then_inc(s_dtl, 16)
                    act_mod(act, range(AHEAD))
                    act_xbc(act, 0, 0)
                    for r in (1, 2):
                        act_pad(act, r, 0)
                        act_mod(act, range(ROWS[r - 1] + AHEAD, ROWS[r] + AHEAD))
                        act_xbc(act, r, 0)
                    act_mod(act, range(ROWS[2] + AHEAD, ROWS[3] + AHEAD))
                    with act.Fori(1, NB) as it:
                        for r in range(3):
                            act_pad(act, r, it)
                            act_xbc(act, r, it)
                    act.wait_ge(s_dtl, 48)
                    act.activation(acol[:], acol[:], ACT.Exp).then_inc(s_de, 1)
                    act.wait_ge(s_wm2u[2], 2 * KT // 4)
                    act.wait_ge(s_dtp, 1)
                    act.activation(sq[0:H, :], ps[0:H, 3072:4096], ACT.Copy).then_inc(s_dtc, 1)
                    act.wait_ge(s_dx, 1)
                    act.activation(dx[1], dx[1], ACT.Exp).then_inc(s_de, 1)
                    act.wait_ge(s_dx, 2)
                    act.activation(dx[3], dx[2], ACT.Ln).then_inc(s_de, 1)
                    for s, n in ((s_zs, NA), (s_ys, NA), (s_ms, 2), (s_xs, XT)):
                        act.wait_ge(s, 16 * n)

                def dve_centre(dve, n):
                    dve.wait_ge(s_mean, n)
                    dve.wait_ge(s_y, n - 1)
                    dve.tensor_tensor(dd[:], acc[:], ps[:, 3072:4096], ALU.subtract).then_inc(s_d, 1)
                    dve.wait_ge(s_d, n)

                def dve_norm(dve, order, n):
                    dve.wait_ge(s_sd, n)
                    order(dve.reciprocal(sq[:], sq[:]))
                    dve.tensor_tensor(dd[:], dd[:], sq[:], ALU.mult).then_inc(s_nrm, 1)

                def dve_conv(dve, order, it):
                    order(dve.tensor_copy(vcur[:], vecs[:, ds(it, 1), :].rearrange("p a n -> p (a n)")))
                    tile_done(dve, 1, it)
                    dve.wait_ge(s_sig, it + 1)
                    dve.tensor_tensor(u[:, TAPS - 1:], ps[:, 1024:2048], sg[:], ALU.mult).then_inc(s_u, 1)
                    dve.wait_ge(s_u, it + 1)
                    order(dve.tensor_scalar(acc[:], u[:, 0:SEQ], vcur[:, V_TAP:V_TAP + 1], vcur[:, V_CB:V_CB + 1],
                                            ALU.mult, ALU.add))
                    for k in range(1, TAPS):
                        ins = dve.scalar_tensor_tensor(out=acc[:], in0=u[:, k:k + SEQ], scalar=vcur[:, V_TAP + k:V_TAP + k + 1],
                                                       in1=acc[:], op0=ALU.mult, op1=ALU.add)
                        if k < TAPS - 1:
                            order(ins)
                    ins.then_inc(s_conv, 1)
                    dve.wait_ge(s_conv, it + 1)

                def dve_mod(dve, row):
                    b, t, s = row // KT, row % KT, row % 4
                    if t == 0 and b > 0:
                        dve.wait_ge(s_ms, b * 16)
                    dve.wait_ge(s_wm2[s], 16 * (row // 4) + 16)
                    if t == 0:
                        ins = dve.tensor_scalar(macc2[:], mslot[s], cact[:, t:t + 1], None, ALU.mult)
                    else:
                        ins = dve.scalar_tensor_tensor(out=macc2[:], in0=mslot[s], scalar=cact[:, t:t + 1],
                                                       in1=macc2[:], op0=ALU.mult, op1=ALU.add)
                    ins.then_inc(s_wm2u[s], 1)
                    dve.wait_ge(s_wm2u[s], row // 4 + 1)

                def dve_xbc(dve, order, r, it):
                    n = 3 * it + r
                    dve.wait_ge(s_pad, n + 1)
                    dve.wait_ge(s_xo, n)
                    order(dve.tensor_scalar(acc[:], xpad[:, 0:SEQ], vcur3[:, r, V_STAP:V_STAP + 1],
                                            vcur3[:, r, V_SB:V_SB + 1], ALU.mult, ALU.add))
                    for k in range(1, STAPS):
                        ins = dve.scalar_tensor_tensor(out=acc[:], in0=xpad[:, k:k + SEQ],
                                                       scalar=vcur3[:, r, V_STAP + k:V_STAP + k + 1],
                                                       in1=acc[:], op0=ALU.mult, op1=ALU.add)
                        if k < STAPS - 1:
                            order(ins)
                    ins.then_inc(s_cb, 1)
                    dve.wait_ge(s_cb, n + 1)

                @block.vector
                def _(dve):
                    per_it = TAPS + 1
                    for t in range(KT):
                        tmp = (acc, dd)[t % 2]
                        if t >= 2:
                            dve.wait_ge(s_ml, t - 1)
                        dve.tensor_scalar(tmp[:], hT[:, t, :], sc1[:, t:t + 1], sh1[:, t:t + 1],
                                          ALU.mult, ALU.add).then_inc(s_mt, 1)
                        if t >= 1:
                            dve.wait_ge(s_mh, t)
                            dve.tensor_tensor(hl[:, t - 1, :], (acc, dd)[(t - 1) % 2][:], hh[:, t - 1, :].bitcast(F32),
                                              ALU.subtract).then_inc(s_ml, 1)
                    dve.wait_ge(s_mh, KT)
                    dve.tensor_tensor(hl[:, KT - 1, :], dd[:], hh[:, KT - 1, :].bitcast(F32), ALU.subtract).then_inc(s_ml, 1)
                    dve.wait_ge(s_ml, KT)
                    dve.wait_ge(s_pz, 2)
                    order = Order(dve, o_p1)
                    dve_conv(dve, order, 0)
                    first = order.n
                    with dve.Fori(1, NA) as it:
                        order = Order(dve, o_p1, it * per_it - (per_it - first))
                        dve_centre(dve, it)
                        dve_conv(dve, order, it)
                        dve_norm(dve, order, it)
                        assert order.n == per_it
                    order = Order(dve, o_p1, first + (NA - 1) * per_it)
                    dve_centre(dve, NA)
                    per_b = 3 * (STAPS - 1) + 1
                    orderb = Order(dve, o_p1b)
                    orderb(dve.tensor_copy(vcur3[:], vecs[:, 0:3, :]))
                    dve_norm(dve, order, NA)
                    for r in range(3):
                        dve_xbc(dve, orderb, r, 0)
                        for row in range(ROWS[r], ROWS[r + 1]):
                            dve_mod(dve, row)
                    assert orderb.n == per_b
                    with dve.Fori(1, NB) as it:
                        orderb = Order(dve, o_p1b, it * per_b)
                        orderb(dve.tensor_copy(vcur3[:], vecs[:, ds(3 * it, 3), :]))
                        for r in range(3):
                            dve_xbc(dve, orderb, r, it)
                    order = Order(dve, o_p1c)
                    dve.wait_ge(s_dtt, 1)
                    v, e, w, l, m = dx
                    order(dve.tensor_tensor(v, ps[:, 0:TT * H].rearrange("p (j h) -> p j h", h=H),
                                            dtb[:, None, :].broadcast_to((P, TT, H)), ALU.add))
                    order(dve.tensor_scalar(e, v, -1.0, None, ALU.mult))
                    dve.tensor_tensor(e, v, e, ALU.min).then_inc(s_dx, 1)
                    dve.wait_ge(s_de, 2)
                    dve.tensor_scalar(w, e, 1.0, None, ALU.add).then_inc(s_dx, 1)
                    dve.wait_ge(s_dx, 2)
                    dve.wait_ge(s_de, 3)
                    order(dve.tensor_scalar(m, w, 1.0, None, ALU.is_equal))
                    order(dve.scalar_tensor_tensor(out=w, in0=w, scalar=-1.0, in1=m, op0=ALU.add, op1=ALU.add))
                    order(dve.reciprocal(w, w))
                    order(dve.tensor_tensor(l, l, w, ALU.mult))
                    order(dve.tensor_tensor(l, l, m, ALU.add))
                    order(dve.tensor_tensor(l, l, e, ALU.mult))
                    order(dve.scalar_tensor_tensor(out=dtt[:], in0=v, scalar=0.0, in1=l, op0=ALU.max, op1=ALU.add))
                    order(dve.scalar_tensor_tensor(out=da[:], in0=dtt[:], scalar=-1.0,
                                                   in1=acol[:, None, :].broadcast_to((P, TT, H)),
                                                   op0=ALU.mult, op1=ALU.mult))
        ph01.close()
        retire_semaphores()

        ph23 = ExitStack()
        ysh = sb(ph23, "ysh", [P, CT, SEQ], F32R)
        ysl = sb(ph23, "ysl", [P, CT, SEQ], F32R)
        with ExitStack() as st:
            xc = sb(st, "xc", [P, 2, XT, P])
            zc = sb(st, "zc", [P, 2, CT, P])
            tda = sb(st, "tda", [P, H, P])
            css = sb(st, "css", [P, H])
            ecs = sb(st, "ecs", [P, 2, H, P])
            ee = sb(st, "ee", [P, H, P])
            dcol = sb(st, "dcol", [P, H])
            cbm = sb(st, "cbm", [P, 2, P])
            ce = sb(st, "ce", [P, H, P])
            xd = sb(st, "xd", [P, H, HD])
            xdd = sb(st, "xdd", [P, H, HD])
            btok = sb(st, "btok", [P, 2, P])
            hst = sb(st, "hst", [P, H, HD])
            dxv = sb(st, "dxv", [P, CT, P])
            yv = sb(st, "yv", [P, CT, P])
            yn = sb(st, "yn", [P, CT, P])
            ysq = sb(st, "ysq", [P, CT, P])
            rs = sb(st, "rs", [P, 2, P])
            s_ch = [sem(f"chunk_loaded{b}") for b in range(2)]
            s_csb, s_ecs, s_dif, s_ee, s_ops, s_ce, s_yp, s_yr = (
                [sem(f"{n}{g}") for g in range(2)] for n in
                ("csb_done", "ecs_ready", "diff_ready", "decay_ready", "decay_cb_ready", "c_decay_ready", "y_done", "y_read"))
            s_tda, s_cs, s_cbm, s_tr, s_xd, s_bt = (sem("tri_da_ready"), sem("cs_cb_done"), sem("cs_cb_read"),
                                                    sem("x_transposed2"), sem("xd_ready"), sem("b_token_ready"))
            s_xdd, s_dx, s_sp, s_hst = (sem("xdd_ready"), sem("dx_ready"),
                                              sem("states_done"), sem("state_updated"))
            s_yz, s_ysq, s_sum, s_rs, s_yf, s_yh, s_yo = (sem("y_gated"), sem("y_squared"), sem("y_sums_done"), sem("y_std_done"),
                                                          sem("y_normed"), sem("y_rounded"), sem("y_split"))
            s_h0, o_p2 = sem("state_zeroed"), sem("p2_order")
            LOOPED = TT - 2

            def col(a, j):
                return a[:, ds(j, 1), :].rearrange("p a h -> p h a") if not isinstance(j, int) else a[:, j, :, None]

            def toks(a, j):
                return a[:, :, ds(j * P, P)] if not isinstance(j, int) else a[:, :, j * P:(j + 1) * P]

            def half(a, g):
                return a[:, 8 * g:8 * g + 8, :]

            with nc.Block() as block:
                @block.sync
                def _(sp):
                    def load(j, b):
                        cols = ds(j * P, P) if not isinstance(j, int) else slice(j * P, (j + 1) * P)
                        sp.dma_start(xc[:, b, :, :], xbc_d[:, :, cols].rearrange("a p n -> p a n")).then_inc(s_ch[b], 16)
                        sp.dma_start(zc[:, b, :, :], zs_d[:, :, cols].rearrange("a p n -> p a n")).then_inc(s_ch[b], 16)

                    load(0, 0)
                    load(1, 1)
                    with sp.Fori(1, TT // 2) as i:
                        for b in range(2):
                            sp.lower_val((2 * i + b) * (P * 4))
                            sp.wait_ge(s_yz, 2 * i + b - 1)
                            load(2 * i + b, b)

                def pe_operands(pe, j, b):
                    pe.wait_ge(s_ch[b], 16 * (j - b) + 32)
                    pe.wait_ge(s_cbm, j)
                    pe.matmul(ps[:, 3328:3328 + H], tri[:], col(da, j), start=True, stop=True)
                    for g in range(2):
                        pe.matmul(ps[:, 3072 + g * P:3200 + g * P], xc[:, b, 8 + g, :], xc[:, b, 10 + g, :],
                                  start=True, stop=True)
                    if not (isinstance(j, int) and j == 0):
                        pe.wait_ge(s_rs, j - 1)
                    for g in range(2):
                        last = pe.transpose(ps[:, 3584 + g * P:3712 + g * P], xc[:, b, 8 + g, :], ident[:])
                    last.then_inc(s_cs, 1)
                    pe.wait_ge(s_tda, j + 1)
                    for g in range(2):
                        pe.wait_ge(s_yr[g], j)
                        for q in (2 * g, 2 * g + 1):
                            last = pe.matmul(ps[:, 512 * q:512 * q + 512], ones[:],
                                             tda[:, 4 * q:4 * q + 4, :].rearrange("p a b -> p (a b)"), start=True, stop=True)
                        last.then_inc(s_csb[g], 1)
                    pe.wait_ge(s_hst, j)
                    for q in range(CT):
                        last = pe.transpose(ps[:, 2048 + q * P:2048 + (q + 1) * P], xc[:, b, q, :], ident[:])
                    last.then_inc(s_tr, 1)

                def pe_outputs(pe, j):
                    pe.wait_ge(s_hst, j)
                    for g in range(2):
                        pe.wait_ge(s_ops[g], j + 1)
                        pe.wait_ge(s_ce[g], j + 1)
                        for h in range(8 * g, 8 * g + 8):
                            q = h // 2
                            dst = ps[:, h * P:(h + 1) * P]
                            pe.matmul(dst, xd[:, 2 * q:2 * q + 2, :].rearrange("p a b -> p (a b)"), ee[:, h, :],
                                      start=True, stop=False)
                            last = pe.matmul(dst, hst[:, 2 * q:2 * q + 2, :].rearrange("p a b -> p (a b)"), ce[:, h, :],
                                             start=False, stop=True)
                        last.then_inc(s_yp[g], 1)
                    pe.wait_ge(s_xdd, j + 1)
                    pe.wait_ge(s_bt, j + 1)
                    for g in range(2):
                        last = pe.matmul(ps[:, 2048 + 512 * g:2560 + 512 * g], btok[:, g, :],
                                         half(xdd, g).rearrange("p a b -> p (a b)"), start=True, stop=True)
                    last.then_inc(s_sp, 1)

                def pe_sums(pe, j, more):
                    pe.wait_ge(s_ysq, j + 1)
                    pe.wait_ge(s_bt, j + 1 + more)
                    for g in range(2):
                        for q in range(4):
                            last = pe.matmul(ps[:, 3840 + g * P:3968 + g * P], ones[:], ysq[:, 4 * g + q, :],
                                             start=(q == 0), stop=(q == 3))
                    last.then_inc(s_sum, 1)

                @block.tensor
                def _(pe):
                    def step(j, b, more=True):
                        pe_outputs(pe, j)
                        if more:
                            pe_operands(pe, j + 1, 1 - b)
                        pe_sums(pe, j, int(more))

                    pe.wait_ge(s_h0, 1)
                    pe_operands(pe, 0, 0)
                    with pe.Fori(0, LOOPED // 2) as i:
                        step(2 * i, 0)
                        step(2 * i + 1, 1)
                    step(TT - 2, 0)
                    step(TT - 1, 1, more=False)

                @block.gpsimd
                def _(pool):
                    def times_tri(j):
                        pool.wait_ge(s_csb[1], j)
                        pool.tensor_tensor(tda[:], tri[:, None, :].broadcast_to((P, H, P)),
                                           col(da, j).broadcast_to((P, H, P)), ALU.mult).then_inc(s_tda, 1)

                    def operands(j, b):
                        for g in range(2):
                            pool.wait_ge(s_ecs[g], j + 1)
                            pool.tensor_tensor(half(ce, g), ecs[:, b, 8 * g:8 * g + 8, :],
                                               xc[:, b, 10 + g:11 + g, :].broadcast_to((P, 8, P)), ALU.mult).then_inc(s_ce[g], 1)
                        pool.wait_ge(s_xd, j + 1)
                        pool.wait_ge(s_ops[1], j + 1)
                        pool.tensor_tensor(xdd[:], xd[:], dcol[:, :, None].broadcast_to((P, H, HD)), ALU.mult).then_inc(s_xdd, 1)
                        for g in range(2):
                            pool.wait_ge(s_yr[g], j)
                        pool.tensor_tensor(dxv[:], xc[:, b, 0:CT, :],
                                           vecs[:, 0:CT, V_D:V_D + 1].broadcast_to((P, CT, P)), ALU.mult).then_inc(s_dx, 1)

                    def step(j, b, more=True, tri_too=True):
                        if more:
                            operands(j + 1, 1 - b)
                        if tri_too:
                            times_tri(j + 2)
                        pool.wait_ge(s_yh, j + 1)
                        pool.tensor_tensor(toks(ysl, j), yn[:], toks(ysh, j).bitcast(F32), ALU.subtract).then_inc(s_yo, 1)

                    times_tri(0)
                    pool.wait_ge(s_ch[0], 32)
                    operands(0, 0)
                    times_tri(1)
                    with pool.Fori(0, LOOPED // 2) as i:
                        step(2 * i, 0)
                        step(2 * i + 1, 1)
                    step(TT - 2, 0, tri_too=False)
                    step(TT - 1, 1, more=False, tri_too=False)

                @block.scalar
                def _(act):
                    def operands(j, b):
                        act.wait_ge(s_cs, j + 1)
                        act.wait_ge(s_sp, j)
                        act.activation(btok[:].rearrange("p a b -> p (a b)"), ps[:, 3584:3840], ACT.Copy).then_inc(s_bt, 1)
                        for g in range(2):
                            act.wait_ge(s_csb[g], j + 1)
                            act.activation(ecs[:, b, 8 * g:8 * g + 8, :].rearrange("p a b -> p (a b)"),
                                           ps[:, 1024 * g:1024 * g + 1024], ACT.Exp).then_inc(s_ecs[g], 1)
                        for g in range(2):
                            act.wait_ge(s_dif[g], j + 1)
                            act.activation(half(ee, g), half(ee, g), ACT.Exp).then_inc(s_ee[g], 1)

                    def step(j, b, more=True):
                        act.wait_ge(s_yz, j + 1)
                        act.wait_ge(s_sum, j)
                        act.activation(ysq[:], yv[:], ACT.Square).then_inc(s_ysq, 1)
                        if more:
                            operands(j + 1, 1 - b)
                        act.wait_ge(s_sum, j + 1)
                        act.wait_ge(s_yf, j)
                        act.activation(rs[:].rearrange("p a b -> p (a b)"), ps[:, 3840:4096], ACT.Sqrt, bias=epsc[:],
                                       scale=1.0 / (4 * P)).then_inc(s_rs, 1)
                        act.wait_ge(s_yf, j + 1)
                        act.activation(toks(ysh, j), yn[:], ACT.Copy).then_inc(s_yh, 1)

                    operands(0, 0)
                    with act.Fori(0, LOOPED // 2) as i:
                        step(2 * i, 0)
                        step(2 * i + 1, 1)
                    step(TT - 2, 0)
                    step(TT - 1, 1, more=False)

                N_OPER, N_OUT = 5, 6

                @block.vector
                def _(dve):
                    def operands(order, j, b):
                        n0 = order.n
                        dve.wait_ge(s_cs, j + 1)
                        order(dve.tensor_copy(css[:], ps[:, 3328:3328 + H]))
                        dve.tensor_tensor(cbm[:], ps[:, 3072:3328].rearrange("p (g l) -> p g l", g=2),
                                          tri[:, None, :].broadcast_to((P, 2, P)), ALU.mult).then_inc(s_cbm, 1)
                        for g in range(2):
                            dve.wait_ge(s_ecs[g], j + 1)
                            order(dve.tensor_tensor(half(ee, g), ps[:, 1024 * g:1024 * g + 1024].rearrange("p (h l) -> p h l", h=8),
                                                    css[:, 8 * g:8 * g + 8, None].broadcast_to((P, 8, P)), ALU.subtract))
                            dve.tensor_scalar(half(ee, g), half(ee, g), 0.0, None, ALU.min).then_inc(s_dif[g], 1)
                        dve.wait_ge(s_tr, j + 1)
                        dve.tensor_tensor(xd[:], ps[:, 2048:3072].rearrange("p (h d) -> p h d", d=HD),
                                          col(dtt, j).broadcast_to((P, H, HD)), ALU.mult).then_inc(s_xd, 1)
                        dve.wait_ge(s_cbm, j + 1)
                        for g in range(2):
                            dve.wait_ge(s_ee[g], j + 1)
                            ins = dve.tensor_copy(dcol[:, 8 * g:8 * g + 8], ee[:, 8 * g:8 * g + 8, P - 1])
                            order(ins)
                            dve.tensor_tensor(half(ee, g), half(ee, g), cbm[:, g:g + 1, :].broadcast_to((P, 8, P)),
                                              ALU.mult).then_inc(s_ops[g], 1)
                        assert order.n - n0 == N_OPER

                    def outputs(order, j, b):
                        for g in range(2):
                            yp = ps[:, 1024 * g:1024 * g + 1024].rearrange("p (q r l) -> p q r l", r=2, l=P)
                            dve.wait_ge(s_yp[g], j + 1)
                            dve.wait_ge(s_dx, j + 1)
                            for r, lo in ((0, 0), (1, HD)):
                                ins = dve.tensor_tensor(yv[lo:lo + HD, 4 * g:4 * g + 4, :], yp[lo:lo + HD, :, r, :],
                                                        dxv[lo:lo + HD, 4 * g:4 * g + 4, :], ALU.add)
                                if r == 0:
                                    order(ins)
                            ins.then_inc(s_yr[g], 1)
                        for g in range(2):
                            dve.wait_ge(s_yr[g], j + 1)
                        dve.tensor_tensor(yv[:], yv[:], zc[:, b, :, :], ALU.mult).then_inc(s_yz, 1)
                        dve.wait_ge(s_hst, j)
                        dve.wait_ge(s_sp, j + 1)
                        order(dve.tensor_tensor(hst[:], hst[:], ecs[:, b, :, P - 1:P].broadcast_to((P, H, HD)), ALU.mult))
                        dve.tensor_tensor(hst[:], hst[:], ps[:, 2048:3072].rearrange("p (h d) -> p h d", d=HD),
                                          ALU.add).then_inc(s_hst, 1)

                    def finish(order, j):
                        dve.wait_ge(s_rs, j + 1)
                        dve.wait_ge(s_yo, j)
                        order(dve.reciprocal(rs[:], rs[:]))
                        for g in range(2):
                            ins = dve.tensor_tensor(yn[:, 4 * g:4 * g + 4, :], yv[:, 4 * g:4 * g + 4, :],
                                                    rs[:, g:g + 1, :].broadcast_to((P, 4, P)), ALU.mult)
                            order(ins)
                        dve.tensor_tensor(yn[:], yn[:], vecs[:, 0:CT, V_SNW:V_SNW + 1].broadcast_to((P, CT, P)),
                                          ALU.mult).then_inc(s_yf, 1)

                    def step(order, j, b, more=True):
                        n0 = order.n
                        outputs(order, j, b)
                        n1 = order.n
                        if more:
                            operands(order, j + 1, 1 - b)
                        n2 = order.n
                        finish(order, j)
                        assert n1 - n0 + order.n - n2 == N_OUT

                    dve.memset(hst[:], 0.0).then_inc(s_h0, 1)
                    dve.wait_ge(s_h0, 1)
                    operands(Order(dve, o_p2), 0, 0)
                    both = N_OPER + N_OUT
                    with dve.Fori(0, LOOPED // 2) as i:
                        order = Order(dve, o_p2, i * (2 * both) + N_OPER)
                        step(order, 2 * i, 0)
                        step(order, 2 * i + 1, 1)
                    order = Order(dve, o_p2, N_OPER + LOOPED * both)
                    step(order, TT - 2, 0)
                    step(order, TT - 1, 1, more=False)

        retire_semaphores()

        with ExitStack() as st:
            g1row = sb(st, "g1row", [P, D])
            ych = sb(st, "ych", [P, CT, SEQ], F32R)
            ycl = sb(st, "ycl", [P, CT, SEQ], F32R)
            wraw_o = sb(st, "wraw_o", [P, 4, 512])
            woh = sb(st, "woh", [P, 2, 512], F32R)
            wol = sb(st, "wol", [P, 2, 512], F32R)
            slot3 = sb(st, "slot3", [P, 3, 1024])
            macc3 = sb(st, "macc3", [P, 3, 512])
            bmz = sb(st, "bmz", [P, 3, 512])
            xr = sb(st, "xr", [P, TT, 512])
            tmp = sb(st, "tmp", [P, 512])
            sqj = sb(st, "sqj", [P, 512])
            s_bz, s_bl, s_bu = sem("bias_zeroed"), sem("bias_loaded"), sem("bias_used")
            s_mp, s_row, s_rowd = sem("modp_loaded"), sem("g1_summed"), sem("g1_ready")
            s_yl = [sem(f"y_conv_loaded{s}") for s in range(3)]
            s_yhi, s_ylo = sem("y_conv_rounded"), sem("y_conv_split")
            s_wo = [sem(f"w_out_loaded{s}") for s in range(4)]
            s_wor, s_wos, s_wou = sem("w_out_rounded"), [sem(f"w_out_split{s}") for s in range(2)], [
                sem(f"w_out_used{s}") for s in range(2)]
            s_m3 = [sem(f"wmod3_loaded{s}") for s in range(3)]
            s_m3u = [sem(f"wmod3_summed{s}") for s in range(3)]
            s_ms3, o_p3 = sem("modq_stored"), sem("p3_order")
            s_oa = sem("out_tile_done")
            s_xr = [sem(f"x_tile_loaded{s}") for s in range(TT)]
            s_x1 = [sem(f"x1_stored{s}") for s in range(TT)]
            s_res, s_of, s_sqp = sem("residual_added"), sem("bank_free"), sem("x1_squares_summed")
            wo_v = w_out.rearrange("(t p) n -> p t n", p=P)
            wm3_v = w_mod.rearrange("(p t) n -> p t n", t=KT)
            KORD = list(range(CT, 2 * CT)) + list(range(CT))
            with nc.Block() as block:
                @block.sync
                def _(sp):
                    for q in range(2):
                        sp.dma_start(slot3[:, q, :], modp_d[q, :, :]).then_inc(s_mp, 16)
                    sp.dma_start(g1row[:], bcast(b_mod[:, 2 * D:3 * D], D)).then_inc(s_mp, 16)
                    with sp.Fori(0, 4) as n:
                        for i, k in enumerate(KORD):
                            sp.lower_val((n * 512 + k * (P * D)) * 4)
                            sp.wait_ge(s_wos[i % 2], 8 * n + max(0, i // 2 - 1))
                            sp.dma_start(wraw_o[:, i % 4, :], wo_v[:, k, ds(n * 512, 512)]).then_inc(s_wo[i % 4], 16)

                @block.gpsimd
                def _(pool):
                    with pool.Fori(0, 4) as n:
                        for i in range(KT):
                            s = i % 2
                            pool.wait_ge(s_wo[i % 4], 64 * n + 16 * (i // 4) + 16)
                            pool.wait_ge(s_wou[s], 8 * n + i // 2)
                            pool.tensor_tensor(woh[:, s, :].rearrange("p (a b) -> p a b", b=P),
                                               wraw_o[:, i % 4, :].rearrange("p (a b) -> p a b", b=P),
                                               ones[:, None, :].broadcast_to((P, 4, P)), ALU.mult).then_inc(s_wor, 1)
                            pool.wait_ge(s_wor, KT * n + i + 1)
                            pool.tensor_tensor(wol[:, s, :], wraw_o[:, i % 4, :], woh[:, s, :].bitcast(F32),
                                               ALU.subtract).then_inc(s_wos[s], 1)

                @block.tensor
                def _(pe):
                    pe.wait_ge(s_mp, 48)
                    for q in range(4):
                        last = pe.matmul(ps[:, 512 * q:512 * q + 512], ones[:],
                                         slot3[:, q // 2, 512 * (q % 2):512 * (q % 2) + 512], start=True, stop=True)
                    last.then_inc(s_row, 1)
                    with pe.Fori(0, 4) as n:
                        for i, k in enumerate(KORD):
                            s = i % 2
                            pe.wait_ge(s_wos[s], 8 * n + i // 2 + 1)
                            yh, yl = (ych, ycl) if k < CT else (ysh, ysl)
                            if k < CT:
                                pe.wait_ge(s_ylo, k + 1)
                            for j in range(TT):
                                if i == 0:
                                    pe.wait_ge(s_of, TT * n + j + 1)
                                for m, (y, w) in enumerate(((yh, woh), (yh, wol), (yl, woh))):
                                    last = pe.matmul(ps[:, 512 * j:512 * j + 512], y[:, k % CT, j * P:(j + 1) * P],
                                                     w[:, s, :], start=(i == 0 and m == 0), stop=(i == KT - 1 and m == 2))
                                if i == KT - 1 and j < TT - 1:
                                    last.then_inc(s_oa, 1)
                            last.then_inc(s_wou[s], 1)

                @block.scalar
                def _(act):
                    act.wait_ge(s_row, 1)
                    for t in range(CT):
                        if t == 0:
                            for k in range(3):
                                act.dma_start(slot3[:, k, :], ycv_d[k, :, :]).then_inc(s_yl[k], 16)
                        act.wait_ge(s_yl[t % 3], 16 * (t // 3 + 1))
                        act.activation(ych[:, t, :], slot3[:, t % 3, :], ACT.Copy).then_inc(s_yhi, 1)
                        if t + 3 < CT:
                            act.wait_ge(s_ylo, t + 1)
                            act.dma_start(slot3[:, t % 3, :], ycv_d[t + 3, :, :]).then_inc(s_yl[t % 3], 16)
                    act.wait_ge(s_ylo, CT)
                    act.wait_ge(s_bz, 1)
                    with act.Fori(0, 4) as n:
                        act.lower_val(n * (512 * 4))
                        act.wait_ge(s_bu, 3 * n)
                        act.dma_start(bmz[0:1, :, :], b_mod[:, 3 * D:6 * D].rearrange("a (v n) -> a v n", v=3)[:, :, ds(n * 512, 512)]
                                      ).then_inc(s_bl, 16)
                        act.wait_ge(s_sqp, TT * n)
                        for s in range(TT):
                            act.lower_val(n * (512 * 4))
                            act.wait_ge(s_x1[s], 16 * n)
                            act.dma_start(xr[:, s, :], x[s * P:(s + 1) * P, ds(n * 512, 512)]).then_inc(s_xr[s], 16)
                        for v in range(3):
                            for q in range(KT // 2):
                                i = (KT // 2) * v + q
                                act.lower_val(n * (512 * 4))
                                act.wait_ge(s_m3u[i % 3], 8 * n + i // 3)
                                act.dma_start(slot3[:, i % 3, :].rearrange("p (t n) -> p t n", t=2),
                                              wm3_v[:, 2 * q:2 * q + 2, ds(n * 512 + (3 + v) * D, 512)]).then_inc(s_m3[i % 3], 16)
                        for v in range(3):
                            i = (KT // 2) * v + 7
                            act.lower_val(n * (512 * 4))
                            act.wait_ge(s_m3u[i % 3], 8 * n + i // 3 + 1)
                            act.dma_start(modq_d[v, :, ds(n * 512, 512)], macc3[:, v, :]).then_inc(s_ms3, 16)
                        for j in range(TT):
                            act.lower_val(n * (512 * 4))
                            act.wait_ge(s_res, TT * n + j + 1)
                            act.dma_start(x1_d[j * P:(j + 1) * P, ds(n * 512, 512)], xr[:, j, :]).then_inc(s_x1[j], 16)
                            act.wait_ge(s_sqp, TT * n + j)
                            act.activation(sqj[:], xr[:, j, :], ACT.Square,
                                           accum_out=ssqp[:, j, ds(n, 1)]).then_inc(s_sqp, 1)
                    for s in range(TT):
                        act.wait_ge(s_x1[s], 16 * 4)
                    act.wait_ge(s_ms3, 3 * 4 * 16)

                @block.vector
                def _(dve):
                    dve.memset(bmz[:], 0.0).then_inc(s_bz, 1)
                    dve.wait_ge(s_bz, 1)
                    dve.wait_ge(s_mp, 48)
                    dve.wait_ge(s_row, 1)
                    dve.tensor_tensor(g1row[:], ps[:, 0:D], g1row[:], ALU.add).then_inc(s_rowd, 1)
                    dve.wait_ge(s_rowd, 1)
                    dve.memset(tmp[:], 0.0).then_inc(s_of, TT)
                    for t in range(CT):
                        dve.wait_ge(s_yhi, t + 1)
                        dve.tensor_tensor(ycl[:, t, :], slot3[:, t % 3, :], ych[:, t, :].bitcast(F32),
                                          ALU.subtract).then_inc(s_ylo, 1)
                    dve.wait_ge(s_of, TT)
                    with dve.Fori(0, 4) as n:
                        order = Order(dve, o_p3, n * (3 * (KT // 2 - 1)))
                        dve.wait_ge(s_bl, 16 * n + 16)
                        dve.wait_ge(s_ms3, 48 * n)
                        for v in range(3):
                            for q in range(KT // 2):
                                i = (KT // 2) * v + q
                                dve.wait_ge(s_m3[i % 3], 128 * n + 16 * (i // 3) + 16)
                                w0, w1 = slot3[:, i % 3, 0:512], slot3[:, i % 3, 512:1024]
                                if q == 0:
                                    dve.scalar_tensor_tensor(out=macc3[:, v, :], in0=w0, scalar=cact[:, 0:1], in1=bmz[:, v, :],
                                                             op0=ALU.mult, op1=ALU.add).then_inc(s_bu, 1)
                                    dve.wait_ge(s_bu, 3 * n + v + 1)
                                else:
                                    order(dve.scalar_tensor_tensor(out=macc3[:, v, :], in0=w0, scalar=cact[:, 2 * q:2 * q + 1],
                                                                   in1=macc3[:, v, :], op0=ALU.mult, op1=ALU.add))
                                dve.scalar_tensor_tensor(out=macc3[:, v, :], in0=w1, scalar=cact[:, 2 * q + 1:2 * q + 2],
                                                         in1=macc3[:, v, :], op0=ALU.mult, op1=ALU.add).then_inc(s_m3u[i % 3], 1)
                                dve.wait_ge(s_m3u[i % 3], 8 * n + i // 3 + 1)
                        assert order.n == 3 * (KT // 2 - 1)
                        for j in range(TT):
                            if j < TT - 1:
                                dve.wait_ge(s_oa, (TT - 1) * n + j + 1)
                            else:
                                dve.wait_ge(s_wou[1], 8 * n + 8)
                            dve.wait_ge(s_res, TT * n + j)
                            dve.tensor_tensor(tmp[:], ps[:, 512 * j:512 * j + 512], g1row[:, ds(n * 512, 512)],
                                              ALU.mult).then_inc(s_of, 1)
                            dve.wait_ge(s_of, TT * n + j + TT + 1)
                            dve.wait_ge(s_xr[j], 16 * n + 16)
                            dve.tensor_tensor(xr[:, j, :], xr[:, j, :], tmp[:], ALU.add).then_inc(s_res, 1)
        ph23.close()

        g2row = sb(top, "g2row", [P, D])
        xf = sb(top, "xf", [P, 2, D])
        frow = sb(top, "frow", [P, D])
        ph24 = ExitStack()
        rex = sb(ph24, "rex", [P, TT, E])
        with ExitStack() as st:
            x1s = sb(st, "x1s", [P, TT, D])
            mq = sb(st, "mq", [P, 3, D])
            rows = sb(st, "rows", [P, 2, D])
            nrow = sb(st, "nrow", [P, D])
            ssq2 = sb(st, "ssq2", [P, TT])
            std2 = sb(st, "std2", [P, TT])
            rst2 = sb(st, "rst2", [P, TT])
            h2c = sb(st, "h2c", [P, 2, D])
            h2T = sb(st, "h2T", [P, KT, P])
            wr = sb(st, "wr", [P, KT, E])
            MORD = (1, 0, 2)
            s_mq = [sem(f"modq_loaded{v}") for v in range(3)]
            s_mr, s_mrd = sem("mod_rows_summed"), sem("mod_rows_ready")
            s_nr, s_wr = sem("norm2_w_loaded"), sem("w_router_loaded")
            s_xt = [sem(f"x1_loaded{b}") for b in range(2)]
            s_sq2, s_std2, s_h2, s_h2t, s_h2e, s_lg, s_rex, o_p4 = (
                sem("x1_squared"), sem("x1_std"), sem("h2_ready"), sem("h2_transposed"), sem("h2_evacuated"),
                sem("logits_done"), sem("logits_exp"), sem("p4_order"))
            s_h2s, s_scr = [sem(f"h2_stored{b}") for b in range(2)], sem("scale_row_ready")
            with nc.Block() as block:
                @block.sync
                def _(sp):
                    def x_tile(j):
                        if j >= 2:
                            sp.wait_ge(s_xt[j % 2], 16 * (j // 2))
                        sp.dma_start(x1s[:, j, :], x1_d[j * P:(j + 1) * P, :]).then_inc(s_xt[j % 2], 16)

                    for v in MORD[:2]:
                        sp.dma_start(mq[:, v, :], modq_d[v, :, :]).then_inc(s_mq[v], 16)
                        if v == 1:
                            sp.dma_start(nrow[:], bcast(norm2_w, D)).then_inc(s_nr, 16)
                    x_tile(0)
                    sp.dma_start(wr[:], w_router.rearrange("(p t) e -> p t e", t=KT)).then_inc(s_wr, 16)
                    x_tile(1)
                    sp.dma_start(mq[:, 2, :], modq_d[2, :, :]).then_inc(s_mq[2], 16)
                    for j in range(2, TT):
                        x_tile(j)

                @block.scalar
                def _(act):
                    act.wait_ge(s_sq2, 1)
                    act.activation(std2[:], ssq2[:], ACT.Sqrt, bias=epsc[:], scale=1.0 / D).then_inc(s_std2, 1)
                    for n, dst in ((1, rows[:, 0, :]), (2, g2row[:])):
                        act.wait_ge(s_mr, n + 1)
                        act.activation(dst, ps[:, 2048 * (n % 2):2048 * (n % 2) + 2048], ACT.Copy).then_inc(s_mrd, 1)
                    with act.Fori(0, TT // 2) as i:
                        for b in range(2):
                            j = 2 * i + b
                            act.wait_ge(s_lg, j)
                            for q in range(4):
                                act.wait_ge(s_h2t, 4 * j + q + 1)
                                act.activation(h2T[:, 4 * q:4 * q + 4, :].rearrange("p a b -> p (a b)"),
                                               ps[:, 512 * q:512 * q + 512], ACT.Copy).then_inc(s_h2e, 1)
                            act.wait_ge(s_lg, j + 1)
                            act.activation(rex[:, ds(j, 1), :].rearrange("p a e -> p (a e)"), ps[:, 2048:2048 + E],
                                           ACT.Exp, scale=-1.0).then_inc(s_rex, 1)

                @block.gpsimd
                def _(pool):
                    with pool.Fori(0, TT // 2) as i:
                        for b in range(2):
                            pool.lower_val((2 * i + b) * (P * D * 4))
                            pool.wait_ge(s_h2, 2 * i + b + 1)
                            pool.dma_start(h2_d[ds((2 * i + b) * P, P), :], h2c[:, b, :]).then_inc(s_h2s[b], 16)
                    for b in range(2):
                        pool.wait_ge(s_h2s[b], 16 * (TT // 2))

                @block.vector
                def _(dve):
                    order = Order(dve, o_p4)
                    dve.tensor_reduce(ssq2[:], ssqp[:], X, ALU.add).then_inc(s_sq2, 1)
                    dve.wait_ge(s_nr, 16)
                    dve.wait_ge(s_mr, 1)
                    dve.scalar_tensor_tensor(out=rows[:, 1, :], in0=ps[:, 0:2048], scalar=1.0, in1=nrow[:],
                                             op0=ALU.add, op1=ALU.mult).then_inc(s_scr, 1)
                    dve.wait_ge(s_std2, 1)
                    order(dve.reciprocal(rst2[:], std2[:]))
                    dve.wait_ge(s_scr, 1)
                    dve.wait_ge(s_mrd, 1)
                    with dve.Fori(0, TT // 2) as i:
                        order = Order(dve, o_p4, i * 2 + 1)
                        for b in range(2):
                            j = 2 * i + b
                            dve.wait_ge(s_xt[b], 16 * i + 16)
                            dve.wait_ge(s_h2t, 8 * i)
                            dve.wait_ge(s_h2s[b], 16 * i)
                            order(dve.scalar_tensor_tensor(out=h2c[:, b, :], in0=x1s[:, ds(j, 1), :].rearrange("p a n -> p (a n)"),
                                                           scalar=rst2[:, ds(j, 1)], in1=rows[:, 1, :], op0=ALU.mult, op1=ALU.mult))
                            dve.tensor_tensor(h2c[:, b, :], h2c[:, b, :], rows[:, 0, :], ALU.add).then_inc(s_h2, 1)
                            dve.wait_ge(s_h2, j + 1)

                @block.tensor
                def _(pe):
                    for n, v in enumerate(MORD):
                        pe.wait_ge(s_mq[v], 16)
                        if n == 2:
                            pe.wait_ge(s_scr, 1)
                        for q in range(4):
                            last = pe.matmul(ps[:, 2048 * (n % 2) + 512 * q:2048 * (n % 2) + 512 * q + 512], ones[:],
                                             mq[:, v, 512 * q:512 * q + 512], start=True, stop=True)
                        last.then_inc(s_mr, 1)
                    pe.wait_ge(s_wr, 16)
                    pe.wait_ge(s_mrd, 2)
                    with pe.Fori(0, TT // 2) as i:
                        for b in range(2):
                            j = 2 * i + b
                            pe.wait_ge(s_h2, j + 1)
                            pe.wait_ge(s_h2e, 4 * j)
                            for q in range(4):
                                for a in range(4):
                                    t = 4 * q + a
                                    last = pe.transpose(ps[:, t * P:(t + 1) * P],
                                                        h2c[:, b, :].rearrange("p (m t) -> p t m", t=KT)[:, t, :], ident[:])
                                last.then_inc(s_h2t, 1)
                            pe.wait_ge(s_h2e, 4 * j + 4)
                            pe.wait_ge(s_rex, j)
                            for t in range(KT):
                                last = pe.matmul(ps[:, 2048:2048 + E], h2T[:, t, :], wr[:, t, :],
                                                 start=(t == 0), stop=(t == KT - 1))
                            last.then_inc(s_lg, 1)

        ph56 = ExitStack()
        NP, NRAW, NSPL = 12, 6, 4
        wraw = sb(ph56, "wraw", [P, NRAW, D])
        s_we = [sem(f"expert_w_loaded{s}") for s in range(NRAW)]
        we_g = w_gate.rearrange("e (p t) f -> e p t f", t=KT)
        we_u = w_up.rearrange("e (p t) f -> e p t f", t=KT)
        we_d = w_down.rearrange("e (p t) n -> e p t n", t=FT)

        def load_piece(sp, e, s):
            q = s % 4
            src = (we_g if s < 4 else we_u)[ds(e, 1), :, 4 * q:4 * q + 4, :].rearrange(
                "a p t f -> (a p) (t f)") if s < 8 else we_d[ds(e, 1), :, q, :].rearrange("a p n -> (a p) n")
            sp.dma_start(wraw[:, s % NRAW, :], src).then_inc(s_we[s % NRAW], 16)

        with ExitStack() as st:
            def t3(name, a, b=None):
                return sb(st, name, [P, a] if b is None else [P, a, b])
            sgm, sel, msk, wv, o1, o2, ab = (t3(n, TT, E) for n in ("sgm", "sel", "msk", "wv", "o1", "o2", "ab"))
            q1, q2, q3, q4, gs, keep = (t3(n, TT, G) for n in ("q1", "q2", "q3", "q4", "gs", "keep"))
            r1, r2 = t3("r1", TT), t3("r2", TT)
            biasr = t3("biasr", E)
            iE, iE1 = sb(st, "iE", [P, E], I32), t3("iE1", E)
            wE, w8 = t3("wE", E), t3("w8", G)
            i8 = sb(st, "i8", [P, G], I32)
            i8f, thr = t3("i8f", G), t3("thr", G)
            ip, pf = sb(st, "ip", [P, 1], I32), t3("pf", 1)
            tp = t3("tp", TT, E)
            cnt, incl, st0, nb, binc, val, oh, cmpe = (t3(n, E) for n in
                                                       ("cnt", "incl", "st0", "nb", "binc", "val", "oh", "cmpe"))
            cmp8 = t3("cmp8", E, G)
            df = t3("df", TT, 2)
            eix, stf, tmp1 = t3("eix", 1), t3("stf", 1), t3("tmp1", 1)
            itab, nit = sb(st, "itab", [P, 2], I32), sb(st, "nit", [P, 2], I32)
            ztail = t3("ztail", D)
            ztok = sb(st, "ztok", [P, 1], U32)
            tokid = sb(st, "tokid", [P, TT], U32)
            s_bi, s_io, s_ab, s_pre, s_dest, s_tab = (sem("router_bias_loaded"), sem("iotas_ready"), sem("choices_ready"),
                                                      sem("prefix_done"), sem("dest_ready"), sem("items_ready"))
            s_zt, s_zts, s_its, s_disp, o_p5 = (sem("tail_zeroed"), sem("tail_stored"), sem("items_stored"),
                                                sem("rows_dispatched"), sem("p5_order"))
            with nc.Block() as block:
                @block.sync
                def _(sp):
                    sp.dma_start(biasr[:], row_of(router_bias).broadcast_to((P, E))).then_inc(s_bi, 16)
                    sp.wait_ge(s_zt, 2)
                    sp.dma_start(ybuf_d[2 * SEQ:2 * SEQ + BLK, :], ztail[:]).then_inc(s_zts, 16)
                    sp.dma_start(tok_d[2 * SEQ:2 * SEQ + BLK, :], ztok[:]).then_inc(s_zts, 16)
                    sp.wait_ge(s_tab, 1)
                    sp.dma_start(items_d[:, :], itab[:]).then_inc(s_its, 16)
                    sp.dma_start(nitems_d[:, :], nit[0:1, :]).then_inc(s_its, 16)
                    sp.wait_ge(s_its, 32)
                    e = sp.value_load(items_d[0:1, 0:1], min_val=0, max_val=E - 1)
                    for s in range(NRAW):
                        load_piece(sp, e, s)
                    sp.wait_ge(s_zts, 32)

                @block.gpsimd
                def _(pool):
                    pool.iota(iE[:], [[1, E]], base=0, channel_multiplier=0).then_inc(s_io, 1)
                    pool.iota(i8[:], [[1, G]], base=0, channel_multiplier=0).then_inc(s_io, 1)
                    pool.iota(ip[:], [[0, 1]], base=0, channel_multiplier=1).then_inc(s_io, 1)
                    pool.memset(ztail[:], 0.0).then_inc(s_zt, 1)
                    pool.memset(ztok[:], 0).then_inc(s_zt, 1)
                    pool.iota(tokid[:], [[P, TT]], base=0, channel_multiplier=1).then_inc(s_io, 1)
                    pool.wait_ge(s_dest, 1)
                    for j in range(TT):
                        for k in range(2):
                            pool.indirect_dma_start(out=tok_d[:, :], out_offset=bass.IndirectOffsetOnAxis(ap=dest[:, j, k:k + 1], axis=0),
                                                    in_=tokid[:, j:j + 1], in_offset=None).then_inc(s_disp, 16)
                    pool.wait_ge(s_disp, 2 * TT * 16)

                @block.tensor
                def _(pe):
                    pe.wait_ge(s_ab, 1)
                    rhs = ab[:].rearrange("p a b -> p (a b)")
                    pe.matmul(ps[:, 0:TT * E], tris[:], rhs, start=True, stop=True)
                    pe.matmul(ps[:, 512:512 + TT * E], ones[:], rhs, start=True, stop=True).then_inc(s_pre, 1)

                @block.vector
                def _(dve):
                    order = Order(dve, o_p5)
                    tt = lambda o, a, b, op: order(dve.tensor_tensor(o, a, b, op))
                    ts = lambda o, a, s1, s2, p0, p1=None: order(
                        dve.tensor_scalar(o, a, s1, s2, p0, p1) if p1 is not None else dve.tensor_scalar(o, a, s1, s2, p0))
                    red = lambda o, a, op: order(dve.tensor_reduce(o, a, X, op))
                    dve.wait_ge(s_io, 4)
                    dve.wait_ge(s_bi, 16)
                    order(dve.tensor_copy(iE1[:], iE[:]))
                    order(dve.tensor_copy(i8f[:], i8[:]))
                    order(dve.tensor_copy(pf[:], ip[:]))
                    ts(wE[:], iE1[:], -1.0, float(E), ALU.mult, ALU.add)
                    ts(w8[:], i8f[:], -1.0, float(G), ALU.mult, ALU.add)
                    ts(thr[:], i8f[:], float(BLK), None, ALU.mult)
                    ts(sgm[:], rex[:], 1.0, None, ALU.add)
                    order(dve.reciprocal(sgm[:], sgm[:]))
                    tt(sel[:], sgm[:], biasr[:, None, :].broadcast_to((P, TT, E)), ALU.add)
                    v = sel[:].rearrange("p j (g c) -> p j g c", c=E // G)
                    c4 = [v[:, :, :, n] for n in range(4)]
                    tt(q1[:], c4[0], c4[1], ALU.max)
                    tt(q2[:], c4[0], c4[1], ALU.min)
                    tt(q3[:], c4[2], c4[3], ALU.max)
                    tt(q4[:], c4[2], c4[3], ALU.min)
                    tt(gs[:], q1[:], q3[:], ALU.max)
                    tt(q1[:], q1[:], q3[:], ALU.min)
                    tt(q2[:], q2[:], q4[:], ALU.max)
                    tt(q1[:], q1[:], q2[:], ALU.max)
                    tt(gs[:], gs[:], q1[:], ALU.add)
                    bc = lambda a, n: a[:, :, None].broadcast_to((P, TT, n))
                    red(r1[:], gs[:], ALU.max)
                    tt(keep[:], gs[:], bc(r1, G), ALU.is_equal)
                    tt(keep[:], keep[:], w8[:, None, :].broadcast_to((P, TT, G)), ALU.mult)
                    red(r1[:], keep[:], ALU.max)
                    tt(keep[:], keep[:], bc(r1, G), ALU.is_equal)
                    kb = keep[:, :, :, None].broadcast_to((P, TT, G, E // G))
                    m4 = msk[:].rearrange("p j (g c) -> p j g c", c=E // G)
                    w4 = wv[:].rearrange("p j (g c) -> p j g c", c=E // G)
                    ts(m4, kb, BIG, -BIG, ALU.mult, ALU.add)
                    tt(w4, v, kb, ALU.mult)
                    tt(msk[:], msk[:], wv[:], ALU.add)
                    for o in (o1, o2):
                        red(r1[:], msk[:], ALU.max)
                        tt(wv[:], msk[:], bc(r1, E), ALU.is_equal)
                        tt(wv[:], wv[:], wE[:, None, :].broadcast_to((P, TT, E)), ALU.mult)
                        red(r2[:], wv[:], ALU.max)
                        tt(o[:], wv[:], bc(r2, E), ALU.is_equal)
                        if o is o1:
                            order(dve.scalar_tensor_tensor(out=msk[:], in0=o[:], scalar=-BIG, in1=msk[:], op0=ALU.mult, op1=ALU.add))
                    dve.tensor_tensor(ab[:], o1[:], o2[:], ALU.add).then_inc(s_ab, 1)
                    tt(wv[:], sgm[:], o1[:], ALU.mult)
                    red(gw[:, :, 0], wv[:], ALU.add)
                    tt(wv[:], sgm[:], o2[:], ALU.mult)
                    red(gw[:, :, 1], wv[:], ALU.add)
                    tt(r1[:], gw[:, :, 0], gw[:, :, 1], ALU.add)
                    order(dve.reciprocal(r1[:], r1[:]))
                    tt(gw[:], gw[:], bc(r1, 2), ALU.mult)
                    dve.wait_ge(s_pre, 1)
                    order(dve.memset(tp[:, 0, :], 0.0))
                    for j in range(TT):
                        dst = tp[:, j + 1, :] if j < TT - 1 else cnt[:]
                        tt(dst, ps[:, 512 + E * j:512 + E * (j + 1)], tp[:, j, :], ALU.add)

                    def scan(o, a):
                        order(dve.tensor_tensor_scan(out=o, data0=ones[:, 0:E], data1=a, initial=0.0, op0=ALU.mult, op1=ALU.add))

                    scan(incl[:], cnt[:])
                    tt(st0[:], incl[:], cnt[:], ALU.subtract)
                    tt(tp[:], tp[:], ps[:, 0:TT * E].rearrange("p (j e) -> p j e", e=E), ALU.add)
                    tt(tp[:], tp[:], st0[:, None, :].broadcast_to((P, TT, E)), ALU.add)
                    for k, o in enumerate((o1, o2)):
                        tt(wv[:], tp[:], o[:], ALU.mult)
                        red(df[:, :, k], wv[:], ALU.add)
                    dve.tensor_copy(dest[:], df[:]).then_inc(s_dest, 1)
                    tt(cmp8[:], cnt[:, :, None].broadcast_to((P, E, G)), thr[:, None, :].broadcast_to((P, E, G)), ALU.is_gt)
                    red(nb[:], cmp8[:], ALU.add)
                    scan(binc[:], nb[:])
                    order(dve.tensor_copy(nit[:, 0:1], binc[:, E - 1:E]))
                    ts(tmp1[:], binc[:, E - 1:E], 1.0, None, ALU.subtract)
                    order(dve.tensor_copy(nit[:, 1:2], tmp1[:]))
                    tt(pf[:], pf[:], tmp1[:], ALU.min)
                    ts(cmpe[:], binc[:], pf[:], None, ALU.is_le)
                    red(eix[:], cmpe[:], ALU.add)
                    tt(val[:], binc[:], nb[:], ALU.subtract)
                    order(dve.scalar_tensor_tensor(out=val[:], in0=val[:], scalar=-float(BLK), in1=st0[:], op0=ALU.mult, op1=ALU.add))
                    ts(oh[:], iE1[:], eix[:], None, ALU.is_equal)
                    tt(val[:], val[:], oh[:], ALU.mult)
                    red(stf[:], val[:], ALU.add)
                    order(dve.scalar_tensor_tensor(out=stf[:], in0=pf[:], scalar=float(BLK), in1=stf[:], op0=ALU.mult, op1=ALU.add))
                    order(dve.tensor_copy(itab[:, 0:1], eix[:]))
                    dve.tensor_copy(itab[:, 1:2], stf[:]).then_inc(s_tab, 1)
                    dve.wait_ge(s_tab, 1)

        s_fr, s_xf = sem("final_w_loaded"), [sem(f"x1_reloaded{b}") for b in range(2)]
        with ExitStack() as st:
            whi = sb(st, "whi", [P, NSPL, D], F32R)
            wlo = sb(st, "wlo", [P, NSPL, D], F32R)
            xrow = sb(st, "xrow", [P, D])
            xTn = sb(st, "xTn", [P, KT, P])
            xhi = sb(st, "xhi", [P, KT, P], F32R)
            xlo = sb(st, "xlo", [P, KT, P], F32R)
            gsl = sb(st, "gsl", [P, FE])
            hb = sb(st, "hb", [P, FE])
            hhi = sb(st, "hhi", [P, FT, P], F32R)
            hlo = sb(st, "hlo", [P, FT, P], F32R)
            orow = sb(st, "orow", [P, D])
            tix = sb(st, "tix", [P, 1], U32)
            pace = sb(st, "pace", [P, 1])
            s_wsp = [sem(f"expert_w_split{s}") for s in range(NRAW)]
            s_wu = [sem(f"expert_w_used{s}") for s in range(NSPL)]
            s_whi, s_ti, s_pace = sem("expert_w_rounded"), sem("tokens_loaded"), sem("gather_may_start")
            s_xr2, s_xtr2, s_xte, s_xhi, s_xlo = (sem("rows_loaded"), sem("rows_transposed"), sem("rows_evacuated"),
                                                  sem("rows_rounded"), sem("rows_split"))
            s_gs, s_hb, s_hbt, s_hhi, s_hlo, s_or, s_os = (
                sem("gate_silu"), sem("hidden_ready"), sem("hidden_transposed"), sem("hidden_rounded"),
                sem("hidden_split"), sem("out_rows_ready"), sem("out_rows_stored"))
            def item_count(eng):
                return eng.value_load(nitems_d[0:1, 0:1], min_val=2, max_val=MAX_ITEMS)

            def first_row(eng, i):
                return eng.value_load(items_d[ds(i, 1), 1:2], min_val=0, max_val=2 * SEQ - 1)

            def gather(pool):
                pool.indirect_dma_start(out=xrow[:], out_offset=None, in_=h2_d[:, :],
                                        in_offset=bass.IndirectOffsetOnAxis(ap=tix[:], axis=0)).then_inc(s_xr2, 16)

            with nc.Block() as block:
                @block.sync
                def _(sp):
                    n = item_count(sp)
                    e = sp.value_load(items_d[0:1, 0:1], min_val=0, max_val=E - 1)
                    for s in range(NRAW, NP):
                        sp.wait_ge(s_wsp[s % NRAW], s // NRAW)
                        load_piece(sp, e, s)
                    with sp.Fori(1, n) as i:
                        e = sp.value_load(items_d[ds(i, 1), 0:1], min_val=0, max_val=E - 1)
                        sp.lower_val(e * (D * FE * 4))
                        for s in range(NP):
                            sp.wait_ge(s_wsp[s % NRAW], i * (NP // NRAW) + s // NRAW)
                            load_piece(sp, e, s)
                    sp.dma_start(frow[:], bcast(final_norm_w, D)).then_inc(s_fr, 16)
                    for b in range(2):
                        sp.dma_start(xf[:, b, :], x1_d[b * P:(b + 1) * P, :]).then_inc(s_xf[b], 16)

                @block.gpsimd
                def _(pool):
                    n = item_count(pool)
                    row = pool.value_load(items_d[0:1, 1:2], min_val=0, max_val=2 * SEQ - 1)
                    pool.dma_start(tix[:], tok_d[ds(row, BLK), :]).then_inc(s_ti, 16)
                    pool.wait_ge(s_ti, 16)
                    gather(pool)
                    with pool.Fori(0, n) as i:
                        nxt = first_row(pool, i + 1)
                        pool.wait_ge(s_xr2, 16 * i + 16)
                        pool.dma_start(tix[:], tok_d[ds(nxt, BLK), :]).then_inc(s_ti, 16)
                        pool.wait_ge(s_pace, i)
                        pool.wait_ge(s_ti, 16 * i + 32)
                        pool.wait_ge(s_xtr2, i + 1)
                        pool.tensor_tensor(pace[:], ones[:, 0:1], ones[:, 0:1], ALU.mult).then_inc(s_pace, 1)
                        gather(pool)
                    pool.wait_ge(s_xr2, 16 * n + 16)
                    pool.wait_ge(s_os, 16 * n)

                def transpose_rows(pe, n):
                    pe.wait_ge(s_xr2, 16 * n)
                    for t in range(KT):
                        last = pe.transpose(ps[:, 1024 + t * P:1024 + (t + 1) * P],
                                            xrow[:].rearrange("p (m t) -> p t m", t=KT)[:, t, :], ident[:])
                    last.then_inc(s_xtr2, 1)

                def product(pe, dst, ahi, alo, bhi, blo, first, final):
                    pe.matmul(dst, ahi, bhi, start=first, stop=False)
                    pe.matmul(dst, ahi, blo, start=False, stop=False)
                    return pe.matmul(dst, alo, bhi, start=False, stop=final)

                def split_ready(pe, i, s):
                    pe.wait_ge(s_wsp[s % NRAW], i * (NP // NRAW) + s // NRAW + 1)

                @block.tensor
                def _(pe):
                    n = item_count(pe)
                    transpose_rows(pe, 1)
                    with pe.Fori(0, n) as i:
                        pe.wait_ge(s_xlo, i + 1)
                        for s in range(8):
                            split_ready(pe, i, s)
                            if s == 0:
                                pe.wait_ge(s_gs, i)
                            if s == 4:
                                pe.wait_ge(s_hb, i)
                            for k in range(4):
                                t, w = 4 * (s % 4) + k, slice(FE * k, FE * (k + 1))
                                last = product(pe, ps[:, 512 * (s // 4):512 * (s // 4) + 512], xhi[:, t, :], xlo[:, t, :],
                                               whi[:, s % NSPL, w], wlo[:, s % NSPL, w], t == 0, t == KT - 1)
                            last.then_inc(s_wu[s % NSPL], 1)
                            if s == 5:
                                pe.wait_ge(s_or, i)
                                pe.wait_ge(s_xte, i + 1)
                                transpose_rows(pe, i + 2)
                        pe.wait_ge(s_hb, i + 1)
                        for t in range(FT):
                            last = pe.transpose(ps[:, 3072 + t * P:3072 + (t + 1) * P],
                                                hb[:].rearrange("p (m t) -> p t m", t=FT)[:, t, :], ident[:])
                        last.then_inc(s_hbt, 1)
                        pe.wait_ge(s_xte, i + 2)
                        pe.wait_ge(s_hlo, i + 1)
                        for t in range(FT):
                            s = 8 + t
                            split_ready(pe, i, s)
                            for q in range(4):
                                w = slice(512 * q, 512 * q + 512)
                                last = product(pe, ps[:, 1024 + 512 * q:1536 + 512 * q], hhi[:, t, :], hlo[:, t, :],
                                               whi[:, s % NSPL, w], wlo[:, s % NSPL, w], t == 0, t == FT - 1)
                            last.then_inc(s_wu[s % NSPL], 1)

                def round_w(act, i, s):
                    act.wait_ge(s_we[s % NRAW], i * (16 * (NP // NRAW)) + 16 * (s // NRAW + 1))
                    act.wait_ge(s_wu[s % NSPL], i * (NP // NSPL) + s // NSPL)
                    act.activation(whi[:, s % NSPL, :], wraw[:, s % NRAW, :], ACT.Copy).then_inc(s_whi, 1)

                def take_rows(act, n):
                    act.wait_ge(s_xtr2, n)
                    act.activation(xTn[:].rearrange("p a b -> p (a b)"), ps[:, 1024:3072], ACT.Copy).then_inc(s_xte, 1)

                def put_out(act, i):
                    row = first_row(act, i)
                    act.lower_val(row * (D * 4))
                    act.wait_ge(s_wu[(NP - 1) % NSPL], (i + 1) * (NP // NSPL))
                    act.wait_ge(s_os, 16 * i)
                    act.activation(orow[:], ps[:, 1024:3072], ACT.Copy).then_inc(s_or, 1)
                    act.wait_ge(s_or, i + 1)
                    act.dma_start(ybuf_d[ds(row, BLK), :], orow[:]).then_inc(s_os, 16)

                def act_item(act, i, first):
                    for s in range(4):
                        round_w(act, i, s)
                    if not first:
                        put_out(act, i - 1)
                    for s in range(4, 8):
                        round_w(act, i, s)
                    act.wait_ge(s_wu[3], i * (NP // NSPL) + 1)
                    act.wait_ge(s_hb, i)
                    act.activation(gsl[:], ps[:, 0:512], ACT.Silu).then_inc(s_gs, 1)
                    round_w(act, i, 8)
                    round_w(act, i, 9)
                    act.wait_ge(s_xlo, i + 1)
                    take_rows(act, i + 2)
                    round_w(act, i, 10)
                    act.wait_ge(s_hbt, i + 1)
                    act.activation(hhi[:].rearrange("p a b -> p (a b)"), ps[:, 3072:3584], ACT.Copy).then_inc(s_hhi, 1)
                    round_w(act, i, 11)
                    act.activation(xhi[:], xTn[:], ACT.Copy).then_inc(s_xhi, 1)

                @block.scalar
                def _(act):
                    n = item_count(act)
                    take_rows(act, 1)
                    act.wait_ge(s_xte, 1)
                    act.activation(xhi[:], xTn[:], ACT.Copy).then_inc(s_xhi, 1)
                    act_item(act, 0, True)
                    with act.Fori(1, n) as i:
                        act_item(act, i, False)
                    put_out(act, act.value_load(nitems_d[0:1, 1:2], min_val=1, max_val=MAX_ITEMS - 1))

                def split_w(dve, i, s):
                    dve.wait_ge(s_whi, i * NP + s + 1)
                    dve.tensor_tensor(wlo[:, s % NSPL, :], wraw[:, s % NRAW, :], whi[:, s % NSPL, :].bitcast(F32),
                                      ALU.subtract).then_inc(s_wsp[s % NRAW], 1)

                @block.vector
                def _(dve):
                    n = item_count(dve)
                    dve.wait_ge(s_xhi, 1)
                    dve.tensor_tensor(xlo[:], xTn[:], xhi[:].bitcast(F32), ALU.subtract).then_inc(s_xlo, 1)
                    with dve.Fori(0, n) as i:
                        for s in range(11):
                            split_w(dve, i, s)
                        dve.wait_ge(s_gs, i + 1)
                        dve.wait_ge(s_wu[3], i * (NP // NSPL) + 2)
                        dve.tensor_tensor(hb[:], ps[:, 512:1024], gsl[:], ALU.mult).then_inc(s_hb, 1)
                        dve.wait_ge(s_hhi, i + 1)
                        dve.tensor_tensor(hlo[:].rearrange("p a b -> p (a b)"), ps[:, 3072:3584],
                                          hhi[:].bitcast(F32).rearrange("p a b -> p (a b)"), ALU.subtract).then_inc(s_hlo, 1)
                        split_w(dve, i, 11)
                        dve.wait_ge(s_xhi, i + 2)
                        dve.tensor_tensor(xlo[:], xTn[:], xhi[:].bitcast(F32), ALU.subtract).then_inc(s_xlo, 1)
        ph56.close()
        ph24.close()

        with ExitStack() as st:
            y1 = sb(st, "y1", [P, 2, D])
            y2 = sb(st, "y2", [P, 2, D])
            of = sb(st, "of", [P, 2, D])
            junk3 = sb(st, "junk3", [P, D])
            ssq3 = sb(st, "ssq3", [P, TT])
            rst3 = sb(st, "rst3", [P, TT])
            s_y1 = [sem(f"y_gathered{b}") for b in range(2)]
            s_y1s, s_yg, s_sum3, s_sq3, s_std3, s_of3, o_p7 = (
                sem("y_weighted"), sem("y_combined"), sem("residual_combined"), sem("combined_squared"), sem("combined_std"),
                sem("final_ready"), sem("p7_order"))
            s_out = [sem(f"out_stored{b}") for b in range(2)]

            def weight(j, k):
                return gw[:, ds(j, 1), k:k + 1].rearrange("p a b -> p (a b)") if not isinstance(j, int) else gw[:, j, k:k + 1]

            def column(a, j):
                return a[:, ds(j, 1)] if not isinstance(j, int) else a[:, j:j + 1]

            with nc.Block() as block:
                @block.gpsimd
                def _(pool):
                    def gather(j):
                        b = j % 2
                        for k, y in ((0, y1), (1, y2)):
                            pool.indirect_dma_start(out=y[:, b, :], out_offset=None, in_=ybuf_d[:, :],
                                                    in_offset=bass.IndirectOffsetOnAxis(ap=dest[:, j, k:k + 1], axis=0)
                                                    ).then_inc(s_y1[b], 16)

                    gather(0)
                    gather(1)
                    for j in range(TT):
                        b = j % 2
                        pool.wait_ge(s_xf[b], 16 * (j // 2) + 16)
                        pool.wait_ge(s_yg, j + 1)
                        pool.tensor_tensor(xf[:, b, :], xf[:, b, :], y1[:, b, :], ALU.add).then_inc(s_sum3, 1)
                        if j + 2 < TT:
                            pool.wait_ge(s_sum3, j + 1)
                            gather(j + 2)

                @block.sync
                def _(sp):
                    for j in range(TT):
                        b = j % 2
                        sp.wait_ge(s_of3, j + 1)
                        sp.dma_start(out[j * P:(j + 1) * P, :], of[:, b, :]).then_inc(s_out[b], 16)
                        if j + 2 < TT:
                            sp.dma_start(xf[:, b, :], x1_d[(j + 2) * P:(j + 3) * P, :]).then_inc(s_xf[b], 16)
                    for b in range(2):
                        sp.wait_ge(s_out[b], 16 * (TT // 2))

                @block.scalar
                def _(act):
                    def scale(j, b):
                        act.wait_ge(s_y1[b], 16 * (j - b) + 32)
                        act.activation(y1[:, b, :], y1[:, b, :], ACT.Copy, scale=weight(j, 0)).then_inc(s_y1s, 1)

                    def square(j, b):
                        act.wait_ge(s_sum3, j + 1)
                        act.wait_ge(s_sq3, j)
                        act.activation(junk3[:], xf[:, b, :], ACT.Square, accum_out=column(ssq3, j)).then_inc(s_sq3, 1)
                        act.wait_ge(s_sq3, j + 1)
                        act.activation(column(rst3, j), column(ssq3, j), ACT.Sqrt, bias=epsc[:], scale=1.0 / D).then_inc(s_std3, 1)

                    scale(0, 0)
                    with act.Fori(0, TT // 2 - 1) as i:
                        for b in range(2):
                            scale(2 * i + b + 1, 1 - b)
                            square(2 * i + b, b)
                    scale(TT - 1, 1)
                    square(TT - 2, 0)
                    square(TT - 1, 1)

                @block.vector
                def _(dve):
                    def combine(order, j, b):
                        dve.wait_ge(s_y1s, j + 1)
                        order(dve.scalar_tensor_tensor(out=y1[:, b, :], in0=y2[:, b, :], scalar=weight(j, 1),
                                                       in1=y1[:, b, :], op0=ALU.mult, op1=ALU.add))
                        dve.tensor_tensor(y1[:, b, :], y1[:, b, :], g2row[:], ALU.mult).then_inc(s_yg, 1)

                    def finish(order, j, b):
                        dve.wait_ge(s_std3, j + 1)
                        order(dve.reciprocal(column(rst3, j), column(rst3, j)))
                        dve.wait_ge(s_out[b], 8 * (j - b))
                        dve.scalar_tensor_tensor(out=of[:, b, :], in0=xf[:, b, :], scalar=column(rst3, j),
                                                 in1=frow[:], op0=ALU.mult, op1=ALU.mult).then_inc(s_of3, 1)

                    dve.wait_ge(s_fr, 16)
                    combine(Order(dve, o_p7), 0, 0)
                    with dve.Fori(0, TT // 2 - 1) as i:
                        order = Order(dve, o_p7, i * 4 + 1)
                        for b in range(2):
                            combine(order, 2 * i + b + 1, 1 - b)
                            finish(order, 2 * i + b, b)
                    order = Order(dve, o_p7, 4 * (TT // 2 - 1) + 1)
                    combine(order, TT - 1, 1)
                    finish(order, TT - 2, 0)
                    finish(order, TT - 1, 1)


_INS = ["x", "c", "w_mod", "b_mod", "norm1_w", "w_in", "conv_dw_w", "conv_dw_b", "conv_ln_w", "conv_ln_b",
        "ssd_conv_w", "ssd_conv_b", "a_log", "dt_bias", "d_skip", "ssd_norm_w", "w_out", "norm2_w",
        "w_router", "router_bias", "w_gate", "w_up", "w_down", "final_norm_w"]
_OUT = (1, SEQ, D)


def kernel(**inputs):
    import concourse.bacc as bacc
    from concourse.bass_utils import run_bass_kernel_spmd

    nc = bacc.Bacc("TRN2", target_bir_lowering=False, num_devices=1)
    arrays, args = {}, []
    for name in _INS:
        a = np.ascontiguousarray(inputs[name])
        arrays[f"in_{name}_dram"] = a
        args.append(nc.dram_tensor(f"in_{name}_dram", a.shape, mybir.dt.from_np(a.dtype), kind="ExternalInput").ap())
    args.append(nc.dram_tensor("out_0_dram", _OUT, F32, kind="ExternalOutput").ap())
    hybrid_layer(nc, *args)
    r = run_bass_kernel_spmd(nc, [arrays], core_ids=[0])
    return r.results[0]["out_0_dram"]
```
